# Optimizing a Trainium2 kernel written in Bass

```python
import functools
import jax, jax.numpy as jnp
from jax import lax
import numpy as np

D_MODEL = 1024
BATCH = 1
SEQ = 128
DEPTH = 2
DEC_BATCH = 1
DEC_SEQ = 128
PAST_LEN = 128

GRID_W = 64
CONV_CH = 512
CONV_TAPS = 3
NA_HEADS = 8
HEAD_DIM = 64
NA_WIDTH = NA_HEADS * HEAD_DIM
WIN_ROWS = 8
WIN_COLS = 16
COL_BAND = 2 * WIN_COLS
MIX_WIDTH = CONV_CH + NA_WIDTH
SPLITS = (CONV_CH, 2 * CONV_CH, 3 * CONV_CH, 3 * CONV_CH + NA_WIDTH, 3 * CONV_CH + 2 * NA_WIDTH)
IN_WIDTH = 3 * CONV_CH + 3 * NA_WIDTH
FOURIER_GROUPS = 4
FFN_DENSE = 2816
N_EXPERTS = 8
TOP_K = 2
FFN_EXPERT = 3584
N_EVEN = (DEPTH + 1) // 2
N_ODD = DEPTH // 2
RMS_EPS = 1e-6
NEG_INF = -1e30

kernel_name = 'hybrid_diffusion_prefix_trunk_step'

def rmsnorm(x, g):
    xf = x.astype(jnp.float32)
    y = xf * lax.rsqrt(jnp.mean(xf * xf, axis=-1, keepdims=True) + RMS_EPS)
    return (y * g.astype(jnp.float32)).astype(x.dtype)

def adaln(cvec, w, b):
    m = jax.nn.silu(cvec) @ w + b
    return jnp.split(m[:, None, :], 6, axis=-1)

def short_conv(u, w):
    pad = CONV_TAPS // 2
    n = u.shape[1]
    up = jnp.pad(u, ((0, 0), (pad, pad), (0, 0)))
    y = up[:, 0:n, :] * w[0]
    for j in range(1, CONV_TAPS):
        y = y + up[:, j:j + n, :] * w[j]
    return y

def heads(t):
    b, n, _ = t.shape
    return t.reshape(b, n, NA_HEADS, HEAD_DIM).transpose(0, 2, 1, 3)

def context_attention(q, k, v):
    b, n, _ = q.shape
    qh, kh, vh = heads(q), heads(k), heads(v)
    s = jnp.einsum('bhqd,bhkd->bhqk', qh, kh).astype(jnp.float32) * (HEAD_DIM ** -0.5)
    p = jax.nn.softmax(s, axis=-1).astype(vh.dtype)
    o = jnp.einsum('bhqk,bhkd->bhqd', p, vh)
    return o.transpose(0, 2, 1, 3).reshape(b, n, NA_WIDTH), (kh, vh)

def neighbourhood_attention(q, k, v, rpb, k_ctx, v_ctx):
    b, n, _ = q.shape
    rows = n // GRID_W
    wr = min(WIN_ROWS, rows)
    ncb = GRID_W // WIN_COLS

    def grid(t):
        return t.reshape(b, rows, GRID_W, NA_HEADS, HEAD_DIM).transpose(0, 3, 1, 2, 4)

    qg, kg, vg = grid(q), grid(k), grid(v)
    r = jnp.arange(rows)
    row_idx = jnp.clip(r - wr // 2, 0, rows - wr)[:, None] + jnp.arange(wr)[None, :]
    qcol = jnp.arange(GRID_W).reshape(ncb, WIN_COLS)
    col_start = jnp.clip(qcol - WIN_COLS // 2, 0, GRID_W - WIN_COLS)
    band_idx = (jnp.clip(qcol[:, 0] - WIN_COLS // 2, 0, GRID_W - COL_BAND)[:, None]
                + jnp.arange(COL_BAND)[None, :])
    gi_r = row_idx[:, None, :, None]
    gi_c = band_idx[None, :, None, :]
    k_nb = kg[:, :, gi_r, gi_c]
    v_nb = vg[:, :, gi_r, gi_c]
    q_blk = qg.reshape(b, NA_HEADS, rows, ncb, WIN_COLS, HEAD_DIM)
    scale = HEAD_DIM ** -0.5
    s_loc = jnp.einsum('bhrcqd,bhrcwkd->bhrcqwk', q_blk, k_nb).astype(jnp.float32) * scale
    kcol = band_idx[:, None, :]
    cs = col_start[:, :, None]
    valid = (kcol >= cs) & (kcol < cs + WIN_COLS)
    roff = row_idx - r[:, None] + (WIN_ROWS - 1)
    coff = jnp.clip(kcol - qcol[:, :, None], -(WIN_COLS - 1), WIN_COLS - 1) + (WIN_COLS - 1)
    bias = rpb[:, roff[:, None, None, :, None], coff[None, :, :, None, :]]
    s_loc = jnp.where(valid[:, :, None, :], s_loc + bias[None].astype(jnp.float32), NEG_INF)
    n_loc = wr * COL_BAND
    s_loc = s_loc.reshape(b, NA_HEADS, rows, ncb, WIN_COLS, n_loc)
    s_ctx = jnp.einsum('bhrcqd,bhld->bhrcql', q_blk, k_ctx).astype(jnp.float32) * scale
    p = jax.nn.softmax(jnp.concatenate([s_loc, s_ctx], axis=-1), axis=-1).astype(v.dtype)
    v_loc = v_nb.reshape(b, NA_HEADS, rows, ncb, n_loc, HEAD_DIM)
    o = (jnp.einsum('bhrcqk,bhrckd->bhrcqd', p[..., :n_loc], v_loc)
         + jnp.einsum('bhrcql,bhld->bhrcqd', p[..., n_loc:], v_ctx))
    return o.transpose(0, 2, 3, 4, 1, 5).reshape(b, n, NA_WIDTH)

def mixer_ab(h, w_in, conv_w, w_out, attend):
    a_b, a_c, a_x, q, k, v = jnp.split(h @ w_in, SPLITS, axis=-1)
    y_a = a_b * short_conv(a_c * a_x, conv_w)
    y_b, kv = attend(q, k, v)
    return jnp.concatenate([y_a, y_b], axis=-1) @ w_out, kv

def fourier_mix(h, w_f):
    b, n, d = h.shape
    hg = h.astype(jnp.float32).reshape(b, n, FOURIER_GROUPS, d // FOURIER_GROUPS)
    f = jnp.fft.fft2(hg, axes=(1, 3), norm='ortho').real
    return f.reshape(b, n, d).astype(h.dtype) @ w_f

def swiglu(h, w1, w3, w2):
    return (jax.nn.silu(h @ w1) * (h @ w3)) @ w2

def moe(h, router_w, router_b, w1, w3, w2):
    b, n, d = h.shape
    t = h.reshape(b * n, d)
    logits = (t @ router_w).astype(jnp.float32) + router_b.astype(jnp.float32)
    top_v, top_i = lax.top_k(logits, TOP_K)
    wts = jax.nn.softmax(top_v, axis=-1)
    gates = jnp.sum(jax.nn.one_hot(top_i, N_EXPERTS, dtype=jnp.float32) * wts[..., None], axis=1).astype(t.dtype)
    out = gates[:, 0:1] * swiglu(t, w1[0], w3[0], w2[0])
    for e in range(1, N_EXPERTS):
        out = out + gates[:, e:e + 1] * swiglu(t, w1[e], w3[e], w2[e])
    return out.reshape(b, n, d)

def trunk(x, cvec, attend, ada_w, ada_b, norm1_g, norm2_g, w_in, conv_w, w_out, ffn_w1, ffn_w3, ffn_w2,
          fourier_w, router_w, router_b, moe_w1, moe_w3, moe_w2, final_g):
    kvs = []
    for l in range(DEPTH):
        i = l // 2
        sh1, sc1, g1, sh2, sc2, g2 = adaln(cvec, ada_w[l], ada_b[l])
        h = rmsnorm(x, norm1_g[l]) * (1 + sc1) + sh1
        if l % 2 == 0:
            mix, kv = mixer_ab(h, w_in[i], conv_w[i], w_out[i], functools.partial(attend, i))
            kvs.append(kv)
        else:
            mix = fourier_mix(h, fourier_w[i])
        x = x + g1 * mix
        h = rmsnorm(x, norm2_g[l]) * (1 + sc2) + sh2
        if l % 2 == 0:
            ff = swiglu(h, ffn_w1[i], ffn_w3[i], ffn_w2[i])
        else:
            ff = moe(h, router_w[i], router_b[i], moe_w1[i], moe_w3[i], moe_w2[i])
        x = x + g2 * ff
    return rmsnorm(x, final_g), kvs

def setup_inputs(seed: int = 0) -> dict:
    key = jax.random.key(seed)
    ks = jax.random.split(key, 24)
    nrm = jax.random.normal
    f32 = jnp.float32
    D = D_MODEL
    return {
        'x_prompt': nrm(ks[0], (BATCH, SEQ, D), f32),
        'x_sample': nrm(ks[1], (DEC_BATCH, DEC_SEQ, D), f32),
        'c': nrm(ks[2], (DEC_BATCH, D), f32),
        'cache_k': nrm(ks[3], (DEC_BATCH, N_EVEN, NA_HEADS, PAST_LEN, HEAD_DIM), f32),
        'cache_v': nrm(ks[4], (DEC_BATCH, N_EVEN, NA_HEADS, PAST_LEN, HEAD_DIM), f32),
        'c_ctx': nrm(ks[5], (D,), f32),
        'ada_w': nrm(ks[6], (DEPTH, D, 6 * D), f32) * (0.5 * D ** -0.5),
        'ada_b': nrm(ks[7], (DEPTH, 6 * D), f32) * 0.02,
        'norm1_g': 1.0 + 0.02 * nrm(ks[8], (DEPTH, D), f32),
        'norm2_g': 1.0 + 0.02 * nrm(ks[9], (DEPTH, D), f32),
        'w_in': nrm(ks[10], (N_EVEN, D, IN_WIDTH), f32) * D ** -0.5,
        'conv_w': nrm(ks[11], (N_EVEN, CONV_TAPS, CONV_CH), f32) * CONV_TAPS ** -0.5,
        'rpb': nrm(ks[12], (N_EVEN, NA_HEADS, 2 * WIN_ROWS - 1, 2 * WIN_COLS - 1), f32) * 0.1,
        'w_out': nrm(ks[13], (N_EVEN, MIX_WIDTH, D), f32) * MIX_WIDTH ** -0.5,
        'ffn_w1': nrm(ks[14], (N_EVEN, D, FFN_DENSE), f32) * D ** -0.5,
        'ffn_w3': nrm(ks[15], (N_EVEN, D, FFN_DENSE), f32) * D ** -0.5,
        'ffn_w2': nrm(ks[16], (N_EVEN, FFN_DENSE, D), f32) * FFN_DENSE ** -0.5,
        'fourier_w': nrm(ks[17], (N_ODD, D, D), f32) * D ** -0.5,
        'router_w': nrm(ks[18], (N_ODD, D, N_EXPERTS), f32) * D ** -0.5,
        'router_b': nrm(ks[19], (N_ODD, N_EXPERTS), f32) * 0.01,
        'moe_w1': nrm(ks[20], (N_ODD, N_EXPERTS, D, FFN_EXPERT), f32) * D ** -0.5,
        'moe_w3': nrm(ks[21], (N_ODD, N_EXPERTS, D, FFN_EXPERT), f32) * D ** -0.5,
        'moe_w2': nrm(ks[22], (N_ODD, N_EXPERTS, FFN_EXPERT, D), f32) * FFN_EXPERT ** -0.5,
        'final_g': 1.0 + 0.02 * nrm(ks[23], (D,), f32),
    }

def reference(x_prompt, x_sample, c, cache_k, cache_v, c_ctx, ada_w, ada_b, norm1_g, norm2_g, w_in, conv_w,
              rpb, w_out, ffn_w1, ffn_w3, ffn_w2, fourier_w, router_w, router_b, moe_w1, moe_w3, moe_w2,
              final_g):
    shared = (ada_w, ada_b, norm1_g, norm2_g, w_in, conv_w, w_out, ffn_w1, ffn_w3, ffn_w2,
              fourier_w, router_w, router_b, moe_w1, moe_w3, moe_w2, final_g)

    def ctx_attend(i, q, k, v):
        return context_attention(q, k, v)

    y_prompt, kvs = trunk(x_prompt, c_ctx[None, :], ctx_attend, *shared)
    new_cache_k = jnp.stack([kv[0] for kv in kvs], axis=1)
    new_cache_v = jnp.stack([kv[1] for kv in kvs], axis=1)

    def latent_attend(i, q, k, v):
        return neighbourhood_attention(q, k, v, rpb[i], cache_k[:, i], cache_v[:, i]), None

    y_sample, _ = trunk(x_sample, c, latent_attend, *shared)
    return (y_prompt, y_sample, new_cache_k, new_cache_v)


_drawn_inputs = setup_inputs


def setup_inputs(seed=0):
    import zlib

    import numpy as np

    out = dict(_drawn_inputs(seed))
    spreads = {}
    factors = {'norm1_g': 3.006,
     'norm2_g': 3.89,
     'rpb': 8.0,
     'router_b': 34.416,
     'final_g': 8.403,
     'cache_k': 8.0,
     'cache_v': 8.0}
    for name, (base, spread) in spreads.items():
        noise = np.random.default_rng([zlib.crc32(name.encode()), seed]).standard_normal(out[name].shape)
        drawn = base * np.exp(spread * noise) if base else spread * noise
        out[name] = __import__('jax').numpy.asarray(drawn.astype(out[name].dtype))
    for name, factor in factors.items():
        out[name] = (out[name] * factor).astype(out[name].dtype)
    return out
```

```python
from contextlib import ExitStack

import concourse.bass as bass
from concourse import mybir

F32 = mybir.dt.float32
I32 = mybir.dt.int32
U32 = mybir.dt.uint32
ALU = mybir.AluOpType
ACT = mybir.ActivationFunctionType
AX_X = mybir.AxisListType.X

P = 128
D = 1024
KT = D // P
NG = 2
T = NG * P
HEADS = 8
HD = 64
PAIRS = HEADS // 2
GRID_W = 64
GRID_R = P // GRID_W
WIN_ROWS, WIN_COLS = 8, 16
BIAS_COLS = 2 * WIN_COLS - 1
BIAS_ROWS = 3
CONV_CH = 512
CONV_TAPS = 3
FFN = 2816
EXPERTS = 8
FFE = 3584
EPS = 1e-6
NEG = -1e30
SCALE = HD ** -0.5
FG = 4
FGC = D // FG

UNIT = 4096
COLS = 512
RING = 7
ROT = 4
FFN_SLICES = -(-FFN // COLS)
MOE_SLICES = FFE // COLS
MOE_UNITS = 3 * MOE_SLICES
SLOTS = 96
ROUNDS = -(-T // SLOTS)
A_JOBS = 2 * MOE_SLICES
AUX_JOBS = 8

CONSTS = [("ident", P), ("ones", P), ("mask", P), ("earlier", P), ("slot_ids", SLOTS), ("expert_ids", EXPERTS),
          ("diag", 2 * GRID_W - 1), ("dft_pos", 2 * P), ("dft_cos", 2 * FGC), ("dft_sin", 2 * FGC)]
CONST_AT = {}
_at = 0
for _name, _n in CONSTS:
    CONST_AT[_name] = (_at, _at + _n)
    _at += _n
CONST_N = _at


def unit_plan():
    plan = [("ada0", u) for u in range(4)]
    plan += [("win", u) for u in (3, 4, 5, 1, 2, 0)]
    plan += [("ada0", u) for u in (4, 5)]
    plan += [("wout", 0), ("wout", 1)]
    plan += [("ada0", u) for u in range(6, 12)]
    plan += [("w1", 0), ("w3", 0)]
    for s in range(1, FFN_SLICES):
        plan += [("w1", s), ("w3", s), ("w2", s - 1)]
    plan += [("w2", FFN_SLICES - 1)]
    plan += [("ada1", u) for u in range(6)]
    plan += [("wf", 0), ("wf", 1)]
    plan += [("ada1", u) for u in range(6, 12)]
    return plan


def moe_plan():
    plan = [("w1", 0), ("w3", 0)]
    for s in range(1, MOE_SLICES):
        plan += [("w1", s), ("w3", s), ("w2", s - 1)]
    return plan + [("w2", MOE_SLICES - 1)]


PLAN = unit_plan()
MOE_PLAN = moe_plan()
N_PRE = len(PLAN)


def build(nc, ins, outs, consts):
    with ExitStack() as ctx:
        _build(ctx, nc, ins, outs, consts)


def _build(ctx, nc, ins, outs, consts):
    def sb(name, shape, dt=F32):
        return ctx.enter_context(nc.sbuf_tensor(name, shape, dt))

    def sem(name):
        return ctx.enter_context(nc.semaphore(name))

    ring = sb("ring", [P, RING, UNIT])
    xT = sb("xT", [P, KT, T])
    hT = sb("hT", [P, KT, T])
    tok = sb("tok", [P, NG, D])
    cst = sb("cst", [P, CONST_N])
    vec_rows = sb("vec_rows", [P, 2, P])
    vecA = sb("vecA", [P, P])
    vecB = sb("vecB", [P, 36])
    cond = sb("cond", [P, KT, NG])
    mods = sb("mods", [P, 2, 48, NG])
    coef = sb("coef", [P, 5, KT, NG])
    var = sb("var", [P, T])
    rstd = sb("rstd", [P, T])
    router = sb("router", [P, KT, EXPERTS])
    router_bias = sb("router_bias", [P, EXPERTS])
    rpb_rows = sb("rpb_rows", [HEADS * BIAS_ROWS, BIAS_COLS])
    rpbT = sb("rpbT", [BIAS_COLS, HEADS * BIAS_ROWS])
    small = sb("small", [P, 256])
    idx = sb("idx", [P, NG, 8], U32)
    most = sb("most", [P, 1], I32)
    eps = sb("eps", [P, 1])
    arena = sb("arena", [P, 12800])

    free = [0]

    def region(*shape):
        n = 1
        for s in shape:
            n *= s
        a = arena[:, free[0]:free[0] + n]
        free[0] += n
        names = "abcd"[:len(shape)]
        if len(shape) > 1:
            a = a.rearrange(f"p ({' '.join(names)}) -> p {' '.join(names)}", **dict(zip(names, shape)))
        return a

    qT, kT = region(4, T), region(4, T)
    v_tok = region(NG, COLS)
    k_tok = region(COLS)
    conv_u, conv_c = region(4, T), region(4, T)
    mixT = region(KT, T)
    kc_tok, vc_tok = region(COLS), region(COLS)
    kcT = region(PAIRS, P)
    bias = region(HEADS, P)
    probs, probsT = region(2, 3 * P), region(2, 3 * P)
    free[0] = 0
    ffn_g = region(2, 4, T)
    ffn_silu = region(2, T)
    free[0] = 0
    dftn = region(2, KT, T)
    fT = region(KT, T)
    free[0] = 0
    take = region(NG, EXPERTS, SLOTS)
    give = region(NG, EXPERTS, SLOTS)
    giveT = region(EXPERTS, T)
    hg = region(KT, SLOTS)
    moe_g = region(2, 4, SLOTS)
    moe_silu = region(2, 2 * SLOTS)
    yT = region(KT, SLOTS)
    y_slot = region(D)
    acc = region(KT, T)

    def C(name):
        a, b = CONST_AT[name]
        return cst[:, a:b]

    ident, ones, mask, earlier = C("ident"), C("ones"), C("mask"), C("earlier")
    diag = C("diag")[0:BIAS_COLS]
    dft_pos = C("dft_pos")
    dft_cos = C("dft_cos").rearrange("p (a b) -> p a b", a=2)
    dft_sin = C("dft_sin").rearrange("p (a b) -> p a b", a=2)

    neg_max = small[:, 0:4].rearrange("p (a b) -> p a b", a=2)
    row_max = small[:, 4:8].rearrange("p (a b) -> p a b", a=2)
    row_sum = small[:, 8:12].rearrange("p (a b) -> p a b", a=2)
    row_inv = small[:, 12:16].rearrange("p (a b) -> p a b", a=2)
    logits = small[:, 16:32].rearrange("p (g e) -> p g e", g=NG)
    top = small[:, 32:48].rearrange("p (g e) -> p g e", g=NG)
    idx_f = small[:, 48:64].rearrange("p (g e) -> p g e", g=NG)
    gap = small[:, 64:66]
    gap_exp = small[:, 66:68]
    gate_den = small[:, 68:70]
    gate_1 = small[:, 70:72]
    gate_2 = small[:, 72:74]
    hot_1 = small[:, 80:96].rearrange("p (g e) -> p g e", g=NG)
    hot_2 = small[:, 96:112].rearrange("p (g e) -> p g e", g=NG)
    chosen = small[:, 112:128].rearrange("p (g e) -> p g e", g=NG)
    gates = small[:, 128:144].rearrange("p (g e) -> p g e", g=NG)
    rank = small[:, 144:160].rearrange("p (g e) -> p g e", g=NG)
    counts = small[:, 160:168]
    most_f = small[:, 168:169]

    ps = ctx.enter_context(nc.psum_tensor("ps", [P, 8, 512], F32))

    ring_full = [sem(f"ring_full{i}") for i in range(RING)]
    in_vec, in_const, in_x, in_cache, in_small = (sem(n) for n in ("in_vec", "in_const", "in_x", "in_cache", "in_small"))
    mm_done = sem("mm_done")
    evac_done = sem("evac_done")
    dve_step = sem("dve_step")
    cond_ready = sem("cond_ready")
    sq_done = sem("sq_done")
    var_ready = sem("var_ready")
    std_ready = sem("std_ready")
    h_scaled = sem("h_scaled")
    h_ready = sem("h_ready")
    eps_ready = sem("eps_ready")
    sc_full, sc_free, mx_ready, exp_done = sem("sc_full"), sem("sc_free"), sem("mx_ready"), sem("exp_done")
    p_ready, pt_full, pt_copied, pv_done = sem("p_ready"), sem("pt_full"), sem("pt_copied"), sem("pv_done")
    up_done, silu_done, g_done, down_done = sem("up_done"), sem("silu_done"), sem("g_done"), sem("down_done")
    ffn_added = sem("ffn_added")
    chosen_ready = sem("chosen_ready")
    gap_ready, gap_exp_done = sem("gap_ready"), sem("gap_exp_done")
    acc_zero = sem("acc_zero")
    most_ready = sem("most_ready")
    rank_moved = sem("rank_moved")
    take_built = sem("take_built")
    give_full, give_copied = sem("give_full"), sem("give_copied")
    e_up, e_silu, e_g = sem("e_up"), sem("e_silu"), sem("e_g")
    e_down, e_yT = sem("e_down"), sem("e_yT")
    aux_full, aux_evac = sem("aux_full"), sem("aux_evac")
    moe_added = sem("moe_added")
    y_ready = sem("y_ready")
    out_kv, out_y = sem("out_kv"), sem("out_y")

    def ring_view(slot, kind, n=COLS):
        if kind == "w2":
            return ring[:, slot, 0:n // P * D].rearrange("p (r n) -> p r n", n=D)
        return ring[:, slot, 0:KT * n].rearrange("p (k n) -> p k n", n=n)

    def ffn_cols(s):
        return min(COLS, FFN - s * COLS)

    def unit_cols(kind, u):
        return ffn_cols(u) if kind in ("w1", "w3", "w2") else COLS

    used_up = []
    at_turn = {}

    block = ctx.enter_context(nc.Block())

    @block.tensor
    def _(pe):
        turn = [0]
        signals = [0]
        unit = [0]

        def done(last):
            signals[0] += 1
            last.then_inc(mm_done, 1)

        def bank():
            n = turn[0]
            if n >= ROT:
                pe.wait_ge(evac_done, n - ROT + 1)
            turn[0] += 1
            return ps[:, n % ROT, :]

        def weights(kind):
            n = unit[0]
            unit[0] += 1
            assert PLAN[n][0] == kind, (n, PLAN[n], kind)
            pe.wait_ge(ring_full[n % RING], 16 * (n // RING + 1))
            return ring_view(n % RING, kind, unit_cols(*PLAN[n]))

        def mm(out, lhsT, rhs, first, last, **kw):
            return pe.matmul(out, lhsT, rhs, start=first, stop=last, **kw)

        def transposes(srcs, rows=P):
            b = bank()
            for i, s in enumerate(srcs):
                ins_ = pe.transpose(b[0:s.shape[1], i * s.shape[0]:(i + 1) * s.shape[0]], s, ident[0:s.shape[0], 0:s.shape[0]])
            done(ins_)

        def ada(kind):
            w = weights(kind)
            b = bank()
            for j in range(4):
                for k in range(KT):
                    last = mm(b[:, NG * j:NG * j + NG], w[:, k, j * P:(j + 1) * P], cond[:, k, :], k == 0, k == KT - 1)
            done(last)
            used_up.append((mm_done, signals[0]))

        def project(kind, src, chunk_hook=None):
            w = weights(kind)
            for j in range(4):
                b = bank()
                for k in range(KT):
                    last = mm(b[:, 0:T], w[:, k, j * P:(j + 1) * P], src[:, k, :], k == 0, k == KT - 1)
                done(last)
                if j == 3:
                    used_up.append((mm_done, signals[0]))
                if chunk_hook:
                    chunk_hook()

        def norm_sum(k):
            b = bank()
            for c in range(KT):
                pe.wait_ge(sq_done, KT * k + c + 1)
                last = mm(b[:, 0:T], ones, hT[:, c, :], c == 0, c == KT - 1)
            done(last)

        def h_tokens(src=hT):
            for g in range(NG):
                for half in range(2):
                    transposes([src[:, 4 * half + i, g * P:(g + 1) * P] for i in range(4)])

        pe.wait_ge(in_const, 16)
        pe.wait_ge(in_vec, 16 * 7)
        transposes([vec_rows[0:36, 1, :]])
        transposes([vec_rows[:, 0, :]])
        pe.wait_ge(in_x, 32)
        at_turn["x"] = turn[0]
        for g in range(NG):
            for half in range(2):
                transposes([tok[:, g, (4 * half + i) * P:(4 * half + i + 1) * P] for i in range(4)])
        pe.wait_ge(in_cache, 32)
        transposes([kc_tok[:, i * P:(i + 1) * P] for i in range(4)])
        pe.wait_ge(in_small, 16 * (HEADS + 2))
        transposes([rpb_rows[:]])
        pe.wait_ge(evac_done, turn[0])
        for q in range(4):
            b = bank()
            for i in range(16):
                kc = 16 * q + i
                last = mm(b[0:GRID_W, 24 * i:24 * (i + 1)], diag[:, GRID_W - 1 - kc:2 * GRID_W - 1 - kc], rpbT[:],
                          True, True)
            done(last)
        norm_sum(0)
        pe.wait_ge(cond_ready, 1)
        for _u in range(4):
            ada("ada0")

        pe.wait_ge(h_ready, 16)
        project("win", hT)
        project("win", hT)
        w = weights("win")
        for g in range(NG):
            b = bank()
            for k in range(KT):
                last = mm(b, hT[:, k, g * P:(g + 1) * P], w[:, k, :], k == 0, k == KT - 1)
            done(last)
        used_up.append((mm_done, signals[0]))
        pe.wait_ge(evac_done, turn[0] - 2)
        transposes([kT[:, c, 0:P] for c in range(4)])

        def scores(h):
            if h >= 2:
                pe.wait_ge(sc_free, h - 1)
            b, o, c = ps[:, 4 + h % 2, :], HD * (h % 2), h // 2
            for g in range(NG):
                mm(b[:, g * P:(g + 1) * P], qT[o:o + HD, c, g * P:(g + 1) * P], kT[o:o + HD, c, g * P:(g + 1) * P],
                   True, True)
            mm(b[:, 2 * P:3 * P], qT[o:o + HD, c, P:T], kcT[o:o + HD, c, :], True, True).then_inc(sc_full, 1)

        def turn_probs(h):
            pe.wait_ge(p_ready, h + 1)
            if h >= 2:
                pe.wait_ge(pt_copied, h - 1)
            for i in range(3):
                last = pe.transpose(ps[:, 6 + h % 2, i * P:(i + 1) * P], probs[:, h % 2, i * P:(i + 1) * P], ident)
            last.then_inc(pt_full, 1)

        pv_bank = [None]

        def values(h):
            pe.wait_ge(pt_copied, h + 1)
            if h % 2 == 0:
                pv_bank[0] = bank()
            b, o, c = pv_bank[0], HD * (h % 2), HD * h
            pt = probsT[:, h % 2, :]
            mm(b[o:o + HD, 0:P], v_tok[:, 0, c:c + HD], pt[:, 0:P], True, True)
            mm(b[o:o + HD, P:T], v_tok[:, 1, c:c + HD], pt[:, P:T], True, False)
            last = mm(b[o:o + HD, P:T], vc_tok[:, c:c + HD], pt[:, T:T + P], False, True)
            last.then_inc(pv_done, 1)

        step = [0]

        def attention_step():
            i = step[0]
            step[0] += 1
            if i < HEADS:
                scores(i)
            if 2 <= i < HEADS + 2:
                turn_probs(i - 2)
            if 3 <= i < HEADS + 3 and (i - 3) % 2:
                values(i - 4)
                values(i - 3)

        at_turn["cache"] = turn[0]
        for _u in range(3):
            project("win", hT, attention_step)
        for _u in range(2):
            ada("ada0")
        pe.wait_ge(evac_done, turn[0] - 2)
        at_turn["wout"] = turn[0]
        for _u in range(2):
            project("wout", mixT)
        for _u in range(4):
            ada("ada0")
        norm_sum(1)
        for _u in range(2):
            ada("ada0")

        pe.wait_ge(h_ready, 32)
        ups = [0]

        def up(s):
            w1, w3 = weights("w1"), weights("w3")
            for f in range(ffn_cols(s) // P):
                a = ups[0]
                ups[0] += 1
                if a >= 4:
                    pe.wait_ge(g_done, a - 3)
                b = ps[:, 4 + a % 4, :]
                for n, w in enumerate((w1, w3)):
                    for k in range(KT):
                        last = mm(b[:, n * T:(n + 1) * T], w[:, k, f * P:(f + 1) * P], hT[:, k, :], k == 0, k == KT - 1)
                last.then_inc(up_done, 1)
            used_up.extend([(up_done, ups[0])] * 2)

        def down(s):
            w2 = weights("w2")
            nf = ffn_cols(s) // P
            for f in range(nf):
                pe.wait_ge(g_done, 4 * s + f + 1)
                for o in range(KT):
                    last = mm(ps[:, o // 2, (o % 2) * T:(o % 2 + 1) * T], w2[:, f, o * P:(o + 1) * P],
                              ffn_g[:, s % 2, f, :], s == 0 and f == 0 and o % 2 == 0,
                              s == FFN_SLICES - 1 and f == nf - 1, skip_group_check=True)
            last.then_inc(down_done, 1)
            used_up.append((down_done, s + 1))

        return_to = turn[0]
        up(0)
        for s in range(1, FFN_SLICES):
            up(s)
            if s == 1:
                pe.wait_ge(evac_done, return_to)
            down(s - 1)
        down(FFN_SLICES - 1)

        pe.wait_ge(ffn_added, KT)
        for _u in range(4):
            ada("ada1")
        norm_sum(2)
        for _u in range(2):
            ada("ada1")
        pe.wait_ge(h_ready, 48)
        h_tokens()
        pe.wait_ge(evac_done, turn[0])
        for g in range(NG):
            for cp in range(4):
                b = bank()
                for i in range(2):
                    c = 2 * cp + i
                    last = mm(b[:, i * T:(i + 1) * T], tok[:, g, c * P:(c + 1) * P], dft_pos, True, True)
                done(last)
        pe.wait_ge(evac_done, turn[0])
        for o in range(KT):
            grp, oc = o // 2, o % 2
            b = bank()
            for n, mat in enumerate((dft_cos, dft_sin)):
                for ic in range(2):
                    last = mm(b[:, 0:T], mat[:, ic, oc * P:(oc + 1) * P], dftn[:, n, 2 * grp + ic, :],
                              n == 0 and ic == 0, n == 1 and ic == 1)
            done(last)
        pe.wait_ge(evac_done, turn[0])
        at_turn["wf"] = turn[0]
        for _u in range(2):
            project("wf", fT)
        for _u in range(4):
            ada("ada1")
        norm_sum(3)
        for _u in range(2):
            ada("ada1")

        pe.wait_ge(h_ready, 64)
        b = bank()
        for g in range(NG):
            for k in range(KT):
                last = mm(b[:, EXPERTS * g:EXPERTS * (g + 1)], hT[:, k, g * P:(g + 1) * P], router[:, k, :],
                          k == 0, k == KT - 1)
        done(last)
        h_tokens()
        pe.wait_ge(chosen_ready, 1)
        b = bank()
        mm(b[:, 0:8], earlier, chosen[:, 0, :], True, True)
        mm(b[:, 8:16], earlier, chosen[:, 1, :], True, False)
        mm(b[:, 8:16], ones, chosen[:, 0, :], False, True)
        mm(b[:, 16:24], ones, chosen[:, 0, :], True, False)
        done(mm(b[:, 16:24], ones, chosen[:, 1, :], False, True))
        pe.wait_ge(evac_done, turn[0])

        def turn_give(r):
            pe.wait_ge(take_built, r + 1)
            for q in range(4):
                for i in range(4):
                    e, g = 2 * q + i // 2, i % 2
                    last = pe.transpose(ps[0:SLOTS, q, i * P:(i + 1) * P], give[:, g, e, :], ident)
                last.then_inc(give_full, 1)

        def expert(job, e, r):
            pe.wait_ge(give_copied, 4 * r + 4)

            def ready(i):
                n = N_PRE + i
                pe.wait_ge(ring_full[n % RING], 16 * (n // RING + 1) + 16 * (MOE_UNITS // RING) * job)
                return ring_view(n % RING, MOE_PLAN[i][0])

            def aux(k):
                pe.wait_ge(aux_evac, AUX_JOBS * job + max(k - 1, 0))
                return ps[:, 6 + k % 2, :]

            for q in range(2):
                b = aux(q)
                for i in range(4):
                    c = 4 * q + i
                    for g in range(NG):
                        last = mm(b[:, i * SLOTS:(i + 1) * SLOTS], tok[:, g, c * P:(c + 1) * P],
                                  take[:, g, bass.ds(e, 1), :].rearrange("p o s -> p (o s)"), g == 0, g == NG - 1)
                last.then_inc(aux_full, 1)
            pe.wait_ge(aux_evac, AUX_JOBS * job + 2)

            at = [0]

            def up(s):
                w1, w3 = ready(at[0]), ready(at[0] + 1)
                at[0] += 2
                for half in range(2):
                    a = 2 * s + half
                    pe.wait_ge(e_g, A_JOBS * job + max(a - 3, 0))
                    b = ps[:, 2 + a % 4, :]
                    for n, w in enumerate((w1, w3)):
                        for i in range(2):
                            f = 2 * half + i
                            for k in range(KT):
                                last = mm(b[:, (2 * n + i) * SLOTS:(2 * n + i + 1) * SLOTS],
                                          w[:, k, f * P:(f + 1) * P], hg[:, k, :], k == 0, k == KT - 1)
                    last.then_inc(e_up, 1)

            def down(s):
                w2 = ready(at[0])
                at[0] += 1
                if s == 0:
                    pe.wait_ge(e_yT, 2 * job)
                for f in range(4):
                    if f % 2 == 0:
                        pe.wait_ge(e_g, A_JOBS * job + 2 * s + f // 2 + 1)
                    for o in range(KT):
                        last = mm(ps[:, o // 4, (o % 4) * SLOTS:(o % 4 + 1) * SLOTS], w2[:, f, o * P:(o + 1) * P],
                                  moe_g[:, s % 2, f, :], s == 0 and f == 0 and o % 4 == 0,
                                  s == MOE_SLICES - 1 and f == 3, skip_group_check=True)
                last.then_inc(e_down, 1)

            up(0)
            for s in range(1, MOE_SLICES):
                up(s)
                down(s - 1)
            down(MOE_SLICES - 1)
            for q in range(2):
                pe.wait_ge(e_yT, 2 * job + q + 1)
                b = aux(2 + q)
                for i in range(4):
                    last = pe.transpose(b[0:SLOTS, i * P:(i + 1) * P], yT[:, 4 * q + i, :], ident)
                last.then_inc(aux_full, 1)
            for q in range(4):
                b = aux(4 + q)
                pe.wait_ge(aux_evac, AUX_JOBS * job + 3 + q // 2)
                for i in range(2):
                    c = 2 * q + i
                    last = mm(b[:, i * T:(i + 1) * T], y_slot[0:SLOTS, c * P:(c + 1) * P],
                              giveT[0:SLOTS, bass.ds(e, 1), :].rearrange("p o t -> p (o t)"), True, True)
                last.then_inc(aux_full, 1)

        turn_give(0)
        with pe.Fori(0, EXPERTS) as e:
            expert(e, e, 0)
        most_here = pe.value_load(most[0:1, 0:1], min_val=0, max_val=T)
        with pe.Fori(1, ROUNDS) as r:
            with pe.If(most_here > SLOTS * r):
                turn_give(r)
                with pe.Fori(0, EXPERTS) as e:
                    expert(EXPERTS * r + e, e, r)
        norm_sum(4)
        pe.wait_ge(y_ready, 16)
        at_turn["out"] = turn[0]
        h_tokens()

    @block.sync
    def _(sp):
        dense = {"ada0": ins["ada_w"][0], "ada1": ins["ada_w"][1], "win": ins["w_in"][0], "wout": ins["w_out"][0],
                 "wf": ins["fourier_w"][0], "w1": ins["ffn_w1"][0], "w3": ins["ffn_w3"][0]}
        for n, (kind, u) in enumerate(PLAN):
            slot, cols = n % RING, unit_cols(kind, u)
            if n >= RING:
                sp.wait_ge(*used_up[n - RING])
            if kind == "w2":
                src = ins["ffn_w2"][0][u * COLS:u * COLS + cols, :].rearrange("(r p) n -> p r n", p=P)
            else:
                src = dense[kind][:, u * COLS:u * COLS + cols].rearrange("(k p) n -> p k n", p=P)
            sp.dma_start(ring_view(slot, kind, cols), src).then_inc(ring_full[slot], 16)

        def load_expert(job, e, first=False):
            for i, (kind, s) in enumerate(MOE_PLAN):
                n = N_PRE + i
                slot = n % RING
                if i < RING and first:
                    sp.wait_ge(*used_up[n - RING])
                else:
                    before, (old, t) = (job if i >= RING else job - 1), MOE_PLAN[i - RING]
                    if old == "w2":
                        sp.wait_ge(e_down, MOE_SLICES * before + t + 1)
                    else:
                        sp.wait_ge(e_up, A_JOBS * before + 2 * t + 2)
                if kind == "w2":
                    src = ins["moe_w2"][0, bass.ds(e, 1), s * COLS:(s + 1) * COLS, :]
                    src = src.rearrange("o (r p) n -> p (o r) n", p=P)
                else:
                    src = ins["moe_" + kind][0, bass.ds(e, 1), :, s * COLS:(s + 1) * COLS]
                    src = src.rearrange("o (k p) n -> p (o k) n", p=P)
                sp.dma_start(ring_view(slot, kind), src).then_inc(ring_full[slot], 16)

        load_expert(0, 0, True)
        with sp.Fori(1, EXPERTS) as e:
            load_expert(e, e)
        sp.wait_ge(most_ready, 1)
        most_here = sp.value_load(most[0:1, 0:1], min_val=0, max_val=T)
        with sp.Fori(1, ROUNDS) as r:
            with sp.If(most_here > SLOTS * r):
                with sp.Fori(0, EXPERTS) as e:
                    load_expert(EXPERTS * r + e, e)
        for g, out in enumerate((outs[0], outs[1])):
            sp.wait_ge(evac_done, at_turn["out"] + 2 * g + 2)
            sp.dma_start(out[0], tok[:, g, :]).then_inc(out_y, 16)
        sp.wait_ge(out_y, 32)

    @block.gpsimd
    def _(pool):
        pool.memset(eps[:], EPS).then_inc(eps_ready, 1)
        pool.wait_ge(evac_done, at_turn["cache"])
        for n, src in ((2, k_tok), (3, v_tok[:, 0, :])):
            pool.dma_start(outs[n][0, 0].rearrange("h s d -> s h d"),
                           src.rearrange("s (h d) -> s h d", h=HEADS)).then_inc(out_kv, 16)
        pool.wait_ge(out_kv, 32)
        pool.wait_ge(most_ready, 1)
        pool.memset(acc, 0.0).then_inc(acc_zero, 1)

    @block.scalar
    def _(act):
        for at, name, g in ((0, "c_ctx", None), (8, "c", 0)):
            src = ins[name] if g is None else ins[name][g]
            act.dma_start(vec_rows[at:at + KT, 1, :], src.rearrange("(k p) -> k p", p=P)).then_inc(in_vec, 16)
        act.dma_start(vec_rows[16:24, 1, :], ins["final_g"].rearrange("(k p) -> k p", p=P)).then_inc(in_vec, 16)
        act.dma_start(vec_rows[24:36, 1, :], ins["conv_w"][0].rearrange("j (k p) -> (j k) p", p=P)).then_inc(in_vec, 16)
        act.dma_start(vec_rows[0:96, 0, :], ins["ada_b"].rearrange("l (k p) -> (l k) p", p=P)).then_inc(in_vec, 16)
        act.dma_start(vec_rows[96:112, 0, :], ins["norm1_g"].rearrange("l (k p) -> (l k) p", p=P)).then_inc(in_vec, 16)
        act.dma_start(vec_rows[112:128, 0, :], ins["norm2_g"].rearrange("l (k p) -> (l k) p", p=P)).then_inc(in_vec, 16)
        act.dma_start(cst[:], consts).then_inc(in_const, 16)
        act.dma_start(tok[:, 0, :], ins["x_prompt"][0]).then_inc(in_x, 16)
        act.dma_start(tok[:, 1, :], ins["x_sample"][0]).then_inc(in_x, 16)
        act.dma_start(kc_tok.rearrange("l (h d) -> l h d", h=HEADS),
                      ins["cache_k"][0, 0].rearrange("h l d -> l h d")).then_inc(in_cache, 16)
        act.dma_start(vc_tok.rearrange("l (h d) -> l h d", h=HEADS),
                      ins["cache_v"][0, 0].rearrange("h l d -> l h d")).then_inc(in_cache, 16)
        for h in range(HEADS):
            act.dma_start(rpb_rows[BIAS_ROWS * h:BIAS_ROWS * (h + 1), :],
                          ins["rpb"][0, h, WIN_ROWS - 2:WIN_ROWS + 1, :]).then_inc(in_small, 16)
        act.dma_start(router[:], ins["router_w"][0].rearrange("(k p) e -> p k e", p=P)).then_inc(in_small, 16)
        act.dma_start(router_bias[:], ins["router_b"][0:1, :].to_broadcast([P, EXPERTS])).then_inc(in_small, 16)

        act.wait_ge(evac_done, 1)
        act.activation(cond[:].rearrange("p k v -> p v k"), vecB[:, 0:16].rearrange("p (v k) -> p v k", v=NG),
                       ACT.Silu).then_inc(cond_ready, 1)

        def norm(k, ready, first):
            for c in range(KT):
                act.wait_ge(ready, first + c if first > 0 else -first)
                act.activation(hT[:, c, :], xT[:, c, :], ACT.Square).then_inc(sq_done, 1)
            act.wait_ge(var_ready, k + 1)
            act.activation(var[:], var[:], ACT.Sqrt).then_inc(std_ready, 1)
            if k < 4:
                l, half = k // 2, k % 2
                for c in range(KT):
                    for g in range(NG):
                        act.wait_ge(h_scaled, 16 * k + NG * c + g + 1)
                        dst = hT[:, c, g * P:(g + 1) * P]
                        act.activation(dst, dst, ACT.Identity,
                                       bias=mods[:, l, 24 * half + c, g:g + 1]).then_inc(h_ready, 1)

        norm(0, evac_done, -at_turn["x"] - 4)
        for h in range(HEADS + 1):
            if h < HEADS:
                act.wait_ge(mx_ready, h + 1)
                act.activation(probs[:, h % 2, 0:P], probs[:, h % 2, 0:P], ACT.Exp, bias=neg_max[:, h % 2, 0:1],
                               accum_out=row_sum[:, h % 2, 0:1])
                act.activation(probs[:, h % 2, P:3 * P], probs[:, h % 2, P:3 * P], ACT.Exp,
                               bias=neg_max[:, h % 2, 1:2], accum_out=row_sum[:, h % 2, 1:2]).then_inc(exp_done, 1)
            if h >= 1:
                i = h - 1
                act.wait_ge(pt_full, i + 1)
                if i >= 2:
                    act.wait_ge(pv_done, i - 1)
                act.activation(probsT[:, i % 2, :], ps[:, 6 + i % 2, 0:3 * P], ACT.Copy).then_inc(pt_copied, 1)
        norm(1, evac_done, at_turn["wout"] + 1)
        act.wait_ge(out_kv, 32)
        for a in range(FFN // P):
            act.wait_ge(up_done, a + 1)
            if a >= 2:
                act.wait_ge(g_done, a - 1)
            act.activation(ffn_silu[:, a % 2, :], ps[:, 4 + a % 4, 0:T], ACT.Silu).then_inc(silu_done, 1)
        norm(2, ffn_added, 1)
        norm(3, evac_done, at_turn["wf"] + 1)
        act.wait_ge(gap_ready, 1)
        act.activation(gap_exp, gap, ACT.Exp).then_inc(gap_exp_done, 1)

        def expert(job):
            for i in range(A_JOBS):
                act.wait_ge(e_up, A_JOBS * job + i + 1)
                act.wait_ge(e_g, A_JOBS * job + max(i - 1, 0))
                act.activation(moe_silu[:, i % 2, :], ps[:, 2 + i % 4, 0:2 * SLOTS], ACT.Silu).then_inc(e_silu, 1)
            act.wait_ge(e_down, MOE_SLICES * job + MOE_SLICES)
            for b in range(2):
                act.activation(yT[:, 4 * b:4 * b + 4, :], ps[:, b, 0:4 * SLOTS].rearrange("p (c s) -> p c s", c=4),
                               ACT.Copy).then_inc(e_yT, 1)

        with act.Fori(0, EXPERTS) as e:
            expert(e)
        most_here = act.value_load(most[0:1, 0:1], min_val=0, max_val=T)
        with act.Fori(1, ROUNDS) as r:
            with act.If(most_here > SLOTS * r):
                with act.Fori(0, EXPERTS) as e:
                    expert(EXPERTS * r + e)
        norm(4, moe_added, 1)

    @block.vector
    def _(dve):
        turn = [0]
        signals = [0]
        steps = [0]

        def full(heads=None):
            n = turn[0]
            turn[0] += 1
            if heads is None:
                signals[0] += 1
                dve.wait_ge(mm_done, signals[0])
            else:
                dve.wait_ge(pv_done, heads)
            return ps[:, n % ROT, :]

        def link(ins_):
            steps[0] += 1
            ins_.then_inc(dve_step, 1)
            dve.wait_ge(dve_step, steps[0])

        def copy_turn(dst, view):
            b = full()
            dve.tensor_copy(dst, view(b)).then_inc(evac_done, 1)

        def mod(l, part):
            return mods[:, l, 8 * part:8 * part + 8, :]

        def ada(l, u):
            b = full()
            bias_ = vecA[:, 48 * l + 4 * u:48 * l + 4 * u + 4].rearrange("p (c o) -> p c o", o=1).to_broadcast([P, 4, NG])
            dve.tensor_tensor(mods[:, l, 4 * u:4 * u + 4, :], b[:, 0:8].rearrange("p (c v) -> p c v", c=4), bias_,
                              ALU.add).then_inc(evac_done, 1)

        def coefs(k):
            l, half = k // 2, k % 2
            g = vecA[:, 96 + 16 * half + 8 * l:96 + 16 * half + 8 * l + 8]
            dve.wait_ge(evac_done, turn[0])
            link(dve.scalar_tensor_tensor(coef[:, k, :, :], mod(l, 3 * half + 1), 1.0,
                                          g.rearrange("p (c o) -> p c o", o=1).to_broadcast([P, KT, NG]),
                                          ALU.add, ALU.mult))

        def norm(k):
            b = full()
            dve.tensor_scalar(var[:], b[:, 0:T], 1.0 / D, EPS, ALU.mult, ALU.add).then_inc(evac_done, 1)
            dve.wait_ge(evac_done, turn[0])
            dve.tensor_scalar(small[:, 200:201], var[:, 0:1], 1.0, None, ALU.mult).then_inc(var_ready, 1)
            dve.wait_ge(std_ready, k + 1)
            link(dve.reciprocal(rstd[:], var[:]))
            for c in range(KT):
                for g in range(NG):
                    sl = slice(g * P, (g + 1) * P)
                    scalar = coef[:, k, c, g:g + 1] if k < 4 else vecB[:, 16 + c:17 + c]
                    dve.scalar_tensor_tensor(hT[:, c, sl], xT[:, c, sl], scalar, rstd[:, sl], ALU.mult,
                                             ALU.mult).then_inc(h_scaled if k < 4 else y_ready, 1)

        def residual(l, part):
            for c in range(KT):
                b = full()
                for g in range(NG):
                    sl = slice(g * P, (g + 1) * P)
                    last = dve.scalar_tensor_tensor(xT[:, c, sl], b[:, sl], mods[:, l, 8 * part + c, g:g + 1], xT[:, c, sl],
                                                    ALU.mult, ALU.add)
                last.then_inc(evac_done, 1)

        def h_tokens(dst):
            for g in range(NG):
                for half in range(2):
                    copy_turn(dst[:, g, half * COLS:(half + 1) * COLS], lambda b: b)

        copy_turn(vecB[:], lambda b: b[:, 0:36])
        copy_turn(vecA[:], lambda b: b[:, 0:P])
        for g in range(NG):
            for half in range(2):
                copy_turn(xT[:, 4 * half:4 * half + 4, g * P:(g + 1) * P],
                          lambda b: b.rearrange("p (c t) -> p c t", c=4))
        copy_turn(kcT, lambda b: b.rearrange("p (c t) -> p c t", c=4))
        copy_turn(rpbT[:], lambda b: b[0:BIAS_COLS, 0:24])
        for q in range(4):
            b = full()[:, 0:384].rearrange("p (k h r) -> p h k r", h=HEADS, r=BIAS_ROWS)
            for qr in range(GRID_R):
                rows = slice(qr * GRID_W, (qr + 1) * GRID_W)
                for kr in range(GRID_R):
                    cols = slice(kr * GRID_W + 16 * q, kr * GRID_W + 16 * q + 16)
                    m = mask[0:GRID_W, cols].rearrange("p (o k) -> p o k", o=1).to_broadcast([GRID_W, HEADS, 16])
                    last = dve.tensor_tensor(bias[rows, :, cols], b[0:GRID_W, :, :, kr - qr + 1], m, ALU.add)
            last.then_inc(evac_done, 1)
        b = full()
        dve.tensor_scalar(var[:], b[:, 0:T], 1.0 / D, EPS, ALU.mult, ALU.add).then_inc(evac_done, 1)
        for u in range(4):
            ada(0, u)
        coefs(0)
        dve.tensor_scalar(small[:, 200:201], var[:, 0:1], 1.0, None, ALU.mult).then_inc(var_ready, 1)
        dve.wait_ge(std_ready, 1)
        link(dve.reciprocal(rstd[:], var[:]))
        for c in range(KT):
            for g in range(NG):
                sl = slice(g * P, (g + 1) * P)
                dve.scalar_tensor_tensor(hT[:, c, sl], xT[:, c, sl], coef[:, 0, c, g:g + 1], rstd[:, sl], ALU.mult,
                                         ALU.mult).then_inc(h_scaled, 1)
        for dst in (qT, kT):
            for c in range(4):
                copy_turn(dst[:, c, :], lambda b: b[:, 0:T])
        for g in range(NG):
            copy_turn(v_tok[:, g, :], lambda b: b)
        copy_turn(k_tok, lambda b: b)

        def soften(h):
            dve.wait_ge(sc_full, h + 1)
            if h >= 2:
                dve.wait_ge(pt_full, h - 1)
            b = ps[:, 4 + h % 2, 0:3 * P].rearrange("p (n t) -> p n t", n=3)
            s = probs[:, h % 2, :].rearrange("p (n t) -> p n t", n=3)
            dve.tensor_scalar(s[:, 0:3:2, :], b[:, 0:3:2, :], SCALE, None, ALU.mult)
            dve.scalar_tensor_tensor(s[:, 1, :], b[:, 1, :], SCALE, bias[:, h, :], ALU.mult, ALU.add).then_inc(sc_free, 1)
            dve.wait_ge(sc_free, h + 1)
            dve.reduce_max(row_max[:, h % 2, 0:1], probs[:, h % 2, 0:P], AX_X)
            link(dve.reduce_max(row_max[:, h % 2, 1:2], probs[:, h % 2, P:3 * P], AX_X))
            dve.tensor_scalar(neg_max[:, h % 2, :], row_max[:, h % 2, :], -1.0, None, ALU.mult).then_inc(mx_ready, 1)

        def normalise(h):
            dve.wait_ge(exp_done, h + 1)
            link(dve.reciprocal(row_inv[:, h % 2, :], row_sum[:, h % 2, :]))
            dve.tensor_scalar(probs[:, h % 2, 0:P], probs[:, h % 2, 0:P], row_inv[:, h % 2, 0:1], None, ALU.mult)
            dve.tensor_scalar(probs[:, h % 2, P:3 * P], probs[:, h % 2, P:3 * P], row_inv[:, h % 2, 1:2], None,
                              ALU.mult).then_inc(p_ready, 1)

        def tap(j, c):
            return vecB[:, 24 + 4 * j + c:25 + 4 * j + c]

        def convolve(c):
            u = conv_u[:, c, :].rearrange("p (g t) -> p g t", g=NG)
            y = conv_c[:, c, :].rearrange("p (g t) -> p g t", g=NG)
            link(dve.tensor_scalar(y, u, tap(1, c), None, ALU.mult))
            link(dve.scalar_tensor_tensor(y[:, :, 1:P], u[:, :, 0:P - 1], tap(0, c), y[:, :, 1:P], ALU.mult, ALU.add))
            link(dve.scalar_tensor_tensor(y[:, :, 0:P - 1], u[:, :, 1:P], tap(2, c), y[:, :, 0:P - 1], ALU.mult, ALU.add))

        for i in range(12):
            b = full()
            part, c = i // 4, i % 4
            if part == 0:
                dve.tensor_copy(conv_c[:, c, :], b[:, 0:T]).then_inc(evac_done, 1)
            elif part == 1:
                dve.tensor_tensor(conv_u[:, c, :], b[:, 0:T], conv_c[:, c, :], ALU.mult).then_inc(evac_done, 1)
                dve.wait_ge(evac_done, turn[0])
                convolve(c)
            else:
                dve.tensor_tensor(mixT[:, c, :], b[:, 0:T], conv_c[:, c, :], ALU.mult).then_inc(evac_done, 1)
            if i < HEADS:
                soften(i)
            if 1 <= i < HEADS + 1:
                normalise(i - 1)
            if 3 <= i < HEADS + 3 and (i - 3) % 2:
                dve.tensor_copy(mixT[:, 4 + (i - 3) // 2, :], full(i - 2)[:, 0:T]).then_inc(evac_done, 1)
        for u in (4, 5):
            ada(0, u)
        dve.wait_ge(evac_done, turn[0])
        residual(0, 2)
        for u in range(6, 10):
            ada(0, u)
        coefs(1)
        norm(1)
        for u in (10, 11):
            ada(0, u)
        for a in range(FFN // P):
            s, f = a // 4, a % 4
            dve.wait_ge(silu_done, a + 1)
            dve.tensor_tensor(ffn_g[:, s % 2, f, :], ps[:, 4 + a % 4, T:2 * T], ffn_silu[:, a % 2, :],
                              ALU.mult).then_inc(g_done, 1)
        dve.wait_ge(down_done, FFN_SLICES)
        dve.wait_ge(evac_done, turn[0])
        for c in range(KT):
            for g in range(NG):
                sl = slice(g * P, (g + 1) * P)
                off = (c % 2) * T + g * P
                last = dve.scalar_tensor_tensor(xT[:, c, sl], ps[:, c // 2, off:off + P], mods[:, 0, 40 + c, g:g + 1],
                                                xT[:, c, sl], ALU.mult, ALU.add)
            last.then_inc(ffn_added, 1)
        for u in range(4):
            ada(1, u)
        coefs(2)
        norm(2)
        for u in (4, 5):
            ada(1, u)
        h_tokens(tok)
        dve.wait_ge(out_kv, 32)
        for g in range(NG):
            for cp in range(4):
                copy_turn(dftn[:, :, 2 * cp:2 * cp + 2, g * P:(g + 1) * P].rearrange("p q c n -> p c q n"),
                          lambda b: b.rearrange("p (c q n) -> p c q n", c=2, q=2))
        for o in range(KT):
            copy_turn(fT[:, o, :], lambda b: b[:, 0:T])
        residual(1, 2)
        for u in range(6, 10):
            ada(1, u)
        coefs(3)
        norm(3)
        for u in (10, 11):
            ada(1, u)

        b = full()
        dve.tensor_tensor(logits, b[:, 0:16].rearrange("p (g e) -> p g e", g=NG),
                          router_bias[:].rearrange("p (o e) -> p o e", o=1).to_broadcast([P, NG, EXPERTS]),
                          ALU.add).then_inc(evac_done, 1)
        dve.wait_ge(evac_done, turn[0])
        for g in range(NG):
            last = dve.max(top[:, g, :], logits[:, g, :])
        link(last)
        for g in range(NG):
            last = dve.max_index(idx[:, g, :], top[:, g, :], logits[:, g, :])
        link(last)
        dve.tensor_tensor(gap.rearrange("p (g o) -> p g o", o=1), top[:, :, 1:2], top[:, :, 0:1],
                          ALU.subtract).then_inc(gap_ready, 1)
        link(dve.tensor_copy(idx_f, idx[:]))
        for g in range(NG):
            dve.tensor_scalar(hot_1[:, g, :], C("expert_ids"), idx_f[:, g, 0:1], None, ALU.is_equal)
            last = dve.tensor_scalar(hot_2[:, g, :], C("expert_ids"), idx_f[:, g, 1:2], None, ALU.is_equal)
        link(last)
        dve.tensor_tensor(chosen, hot_1, hot_2, ALU.add).then_inc(chosen_ready, 1)
        dve.wait_ge(gap_exp_done, 1)
        link(dve.tensor_scalar(gate_den, gap_exp, 1.0, None, ALU.add))
        link(dve.reciprocal(gate_1, gate_den))
        link(dve.tensor_tensor(gate_2, gate_1, gap_exp, ALU.mult))
        for g in range(NG):
            last = dve.tensor_scalar(gates[:, g, :], hot_1[:, g, :], gate_1[:, g:g + 1], None, ALU.mult)
        link(last)
        for g in range(NG):
            last = dve.scalar_tensor_tensor(gates[:, g, :], hot_2[:, g, :], gate_2[:, g:g + 1], gates[:, g, :],
                                            ALU.mult, ALU.add)
        link(last)
        h_tokens(tok)
        b = full()
        dve.tensor_copy(counts, b[:, 16:24])
        dve.tensor_copy(rank, b[:, 0:16].rearrange("p (g e) -> p g e", g=NG)).then_inc(evac_done, 1)
        dve.wait_ge(evac_done, turn[0])
        link(dve.reduce_max(most_f, counts, AX_X))
        dve.tensor_copy(most[:], most_f).then_inc(most_ready, 1)

        def build_round(r, later=False):
            if later:
                dve.tensor_scalar(rank, rank, -float(SLOTS), None, ALU.add).then_inc(rank_moved, 1)
                dve.wait_ge(rank_moved, r)
            for g in range(NG):
                for e in range(EXPERTS):
                    dve.tensor_scalar(take[:, g, e, :], C("slot_ids"), rank[:, g, e:e + 1], chosen[:, g, e:e + 1],
                                      ALU.is_equal, ALU.mult)
                    last = dve.tensor_scalar(give[:, g, e, :], C("slot_ids"), rank[:, g, e:e + 1], gates[:, g, e:e + 1],
                                             ALU.is_equal, ALU.mult)
            last.then_inc(take_built, 1)
            for q in range(4):
                dve.wait_ge(give_full, 4 * r + q + 1)
                dve.tensor_copy(giveT[0:SLOTS, 2 * q:2 * q + 2, :],
                                ps[0:SLOTS, q, :].rearrange("p (e t) -> p e t", e=2)).then_inc(give_copied, 1)

        def expert(job):
            def aux(k):
                dve.wait_ge(aux_full, AUX_JOBS * job + k + 1)
                return ps[:, 6 + k % 2, :]

            for q in range(2):
                dve.tensor_copy(hg[:, 4 * q:4 * q + 4, :],
                                aux(q)[:, 0:4 * SLOTS].rearrange("p (c s) -> p c s", c=4)).then_inc(aux_evac, 1)
            for i in range(A_JOBS):
                s, half = i // 2, i % 2
                dve.wait_ge(e_silu, A_JOBS * job + i + 1)
                dve.tensor_tensor(moe_g[:, s % 2, 2 * half:2 * half + 2, :],
                                  ps[:, 2 + i % 4, 2 * SLOTS:4 * SLOTS].rearrange("p (f s) -> p f s", f=2),
                                  moe_silu[:, i % 2, :].rearrange("p (f s) -> p f s", f=2), ALU.mult).then_inc(e_g, 1)
            for q in range(2):
                dve.tensor_copy(y_slot[0:SLOTS, q * COLS:(q + 1) * COLS], aux(2 + q)[0:SLOTS, :]).then_inc(aux_evac, 1)
            for q in range(4):
                a = acc[:, 2 * q:2 * q + 2, :]
                dve.tensor_tensor(a, aux(4 + q).rearrange("p (c t) -> p c t", c=2), a, ALU.add).then_inc(aux_evac, 1)

        build_round(0)
        dve.wait_ge(acc_zero, 1)
        with dve.Fori(0, EXPERTS) as e:
            expert(e)
        most_here = dve.value_load(most[0:1, 0:1], min_val=0, max_val=T)
        with dve.Fori(1, ROUNDS) as r:
            with dve.If(most_here > SLOTS * r):
                build_round(r, True)
                with dve.Fori(0, EXPERTS) as e:
                    expert(EXPERTS * r + e)
        dve.wait_ge(aux_evac, AUX_JOBS * EXPERTS)
        for c in range(KT):
            for g in range(NG):
                sl = slice(g * P, (g + 1) * P)
                last = dve.scalar_tensor_tensor(xT[:, c, sl], acc[:, c, sl], mods[:, 1, 40 + c, g:g + 1], xT[:, c, sl],
                                                ALU.mult, ALU.add)
            last.then_inc(moe_added, 1)
        norm(4)
        h_tokens(tok)


def shape_constants():
    import numpy as np

    out = np.zeros((P, CONST_N), np.float32)

    def put(name, a):
        lo, hi = CONST_AT[name]
        out[:a.shape[0], lo:hi] = a.reshape(a.shape[0], hi - lo)

    i = np.arange(P)
    put("ident", np.eye(P))
    put("ones", np.ones((P, P)))
    col = i % GRID_W
    start = np.clip(col - WIN_COLS // 2, 0, GRID_W - WIN_COLS)[:, None]
    put("mask", np.where((col[None, :] >= start) & (col[None, :] < start + WIN_COLS), 0.0, NEG))
    put("earlier", i[:, None] < i[None, :])
    put("slot_ids", np.tile(np.arange(SLOTS), (P, 1)))
    put("expert_ids", np.tile(np.arange(EXPERTS), (P, 1)))
    u = np.arange(2 * GRID_W - 1)
    z = (np.arange(BIAS_COLS)[:, None] + u[None, :] == WIN_COLS - 1 + GRID_W - 1).astype(np.float32)
    put("diag", z)
    angle = 2 * np.pi * (np.outer(i, i) % P) / P
    put("dft_pos", np.concatenate([np.cos(angle), np.sin(angle)], 1))
    j = np.arange(FGC)
    angle = 2 * np.pi * (np.outer(j, j) % FGC) / FGC
    norm = 1.0 / np.sqrt(P * FGC)
    put("dft_cos", (norm * np.cos(angle)).reshape(2, P, FGC).transpose(1, 0, 2))
    put("dft_sin", (-norm * np.sin(angle)).reshape(2, P, FGC).transpose(1, 0, 2))
    return out


_INS = ["x_prompt", "x_sample", "c", "cache_k", "cache_v", "c_ctx", "ada_w", "ada_b", "norm1_g", "norm2_g", "w_in",
        "conv_w", "rpb", "w_out", "ffn_w1", "ffn_w3", "ffn_w2", "fourier_w", "router_w", "router_b", "moe_w1",
        "moe_w3", "moe_w2", "final_g"]
_OUTS = [((1, P, D), "float32"), ((1, P, D), "float32"), ((1, 1, HEADS, P, HD), "float32"),
         ((1, 1, HEADS, P, HD), "float32")]


def kernel(**inputs):
    import numpy as _np
    import concourse.bacc as _bacc
    from concourse import mybir as _mybir
    from concourse.bass_utils import run_bass_kernel_spmd as _run

    nc = _bacc.Bacc("TRN2", target_bir_lowering=False, num_devices=1)
    arrays, ins, outs = {}, {}, []
    for name in _INS:
        a = _np.ascontiguousarray(inputs[name])
        arrays[f"in_{name}"] = a
        ins[name] = nc.dram_tensor(f"in_{name}", a.shape, _mybir.dt.from_np(a.dtype), kind="ExternalInput").ap()
    table = shape_constants()
    arrays["shape_constants"] = table
    consts = nc.dram_tensor("shape_constants", table.shape, _mybir.dt.float32, kind="ExternalInput").ap()
    for i, (shape, dtype) in enumerate(_OUTS):
        dt = _mybir.dt.from_np(_np.dtype(dtype))
        outs.append(nc.dram_tensor(f"out_{i}", shape, dt, kind="ExternalOutput").ap())
    build(nc, ins, outs, consts)
    r = _run(nc, [arrays], core_ids=[0])
    return tuple(r.results[0][f"out_{i}"] for i in range(len(_OUTS)))
```

```python
from contextlib import ExitStack

import concourse.bass as bass
from concourse import mybir

F32 = mybir.dt.float32
F32R = mybir.dt.float32r
I32 = mybir.dt.int32
U32 = mybir.dt.uint32
ALU = mybir.AluOpType
ACT = mybir.ActivationFunctionType
AX_X = mybir.AxisListType.X

P = 128
D = 1024
KT = D // P
NG = 2
T = NG * P
HEADS = 8
HD = 64
PAIRS = HEADS // 2
GRID_W = 64
GRID_R = P // GRID_W
WIN_ROWS, WIN_COLS = 8, 16
BIAS_COLS = 2 * WIN_COLS - 1
BIAS_ROWS = 3
CONV_CH = 512
CONV_TAPS = 3
FFN = 2816
EXPERTS = 8
FFE = 3584
EPS = 1e-6
NEG = -1e30
SCALE = HD ** -0.5
FG = 4
FGC = D // FG

COLS = 512
HALF = 2048
RAW = 7
STAGE = 3
AHEAD = STAGE - 1
ROT = 4
FFN_SLICES = -(-FFN // COLS)
MOE_SLICES = FFE // COLS
MOE_HALVES = 6 * MOE_SLICES
SLOTS = 128
ROUNDS = T // SLOTS

CONSTS = [("ident", P), ("ones", P), ("mask", P), ("earlier", P), ("slot_ids", SLOTS), ("expert_ids", EXPERTS),
          ("diag", 2 * GRID_W - 1), ("pair_sum", NG)]
DFT_CONSTS = [("dft_pos", 2 * P), ("dft_cos", 2 * FGC), ("dft_sin", 2 * FGC)]


def placed(table):
    at, out = 0, {}
    for name, n in table:
        out[name] = (at, at + n)
        at += n
    return out, at


CONST_AT, CONST_N = placed(CONSTS)
DFT_AT, DFT_N = placed(DFT_CONSTS)


def dense_plan():
    plan = []

    def by_rows(name, u):
        for half in range(2):
            plan.append((name, slice(half * D // 2, (half + 1) * D // 2), slice(u * COLS, (u + 1) * COLS)))

    def by_cols(name, c, n=COLS // 2):
        plan.append((name, slice(0, D), slice(c, c + n)))

    def ada(l, units):
        for u in units:
            by_rows(f"ada{l}", u)

    def project(name, u):
        for half in range(2):
            by_cols(name, u * COLS + half * COLS // 2)

    def down(s):
        for r in range(s * COLS, min((s + 1) * COLS, FFN), COLS // 2):
            plan.append(("w2", slice(r, r + COLS // 2), slice(0, D)))

    ada(0, range(4))
    project("win", 3)
    project("win", 4)
    by_rows("win", 5)
    for u in (1, 2, 0):
        project("win", u)
    ada(0, (4, 5))
    for u in range(2):
        project("wout", u)
    ada(0, range(6, 12))
    for s in range(FFN_SLICES):
        for c in range(s * COLS, min((s + 1) * COLS, FFN), COLS // 2):
            by_cols("w1", c)
            by_cols("w3", c)
        if s:
            down(s - 1)
    down(FFN_SLICES - 1)
    ada(1, range(6))
    for u in range(2):
        project("wf", u)
    ada(1, range(6, 12))
    return plan


def moe_plan():
    plan = []
    for s in range(MOE_SLICES):
        plan += [("w1", s, 0), ("w1", s, 1), ("w3", s, 0), ("w3", s, 1)]
        if s:
            plan += [("w2", s - 1, 0), ("w2", s - 1, 1)]
    return plan + [("w2", MOE_SLICES - 1, 0), ("w2", MOE_SLICES - 1, 1)]


PLAN = dense_plan()
MOE_PLAN = moe_plan()
N_PRE = len(PLAN)
assert MOE_HALVES % RAW == 0 and MOE_HALVES % STAGE == 0 and len(MOE_PLAN) == MOE_HALVES


def build(nc, ins, outs, consts, dft_consts):
    with ExitStack() as ctx:
        _build(ctx, nc, ins, outs, consts, dft_consts)


def _build(ctx, nc, ins, outs, consts, dft_consts):
    def sb(name, shape, dt=F32):
        return ctx.enter_context(nc.sbuf_tensor(name, shape, dt))

    def sem(name):
        return ctx.enter_context(nc.semaphore(name))

    raw = sb("raw", [P, RAW, HALF])
    w_hi = sb("w_hi", [P, STAGE, HALF], F32R)
    w_lo = sb("w_lo", [P, STAGE, HALF], F32R)
    xT = sb("xT", [P, KT, T])
    hT = sb("hT", [P, KT, T])
    tok = sb("tok", [P, NG, D])
    cst = sb("cst", [P, CONST_N])
    vec_rows = sb("vec_rows", [P, 2, P])
    vecA = sb("vecA", [P, P])
    vecB = sb("vecB", [P, 36])
    cond = sb("cond", [P, KT, NG])
    cond_r = sb("cond_r", [P, 4 * KT + P], F32R)
    mods = sb("mods", [P, 2, 48, NG])
    coef = sb("coef", [P, 4, KT, NG])
    var = sb("var", [P, T])
    rstd = sb("rstd", [P, T])
    router = sb("router", [P, KT, EXPERTS])
    router_bias = sb("router_bias", [P, EXPERTS])
    rpb_rows = sb("rpb_rows", [HEADS * BIAS_ROWS, BIAS_COLS])
    rpbT = sb("rpbT", [BIAS_COLS, HEADS * BIAS_ROWS])
    small = sb("small", [P, 176])
    idx = sb("idx", [P, NG, 8], U32)
    most = sb("most", [P, 1], I32)
    arena = sb("arena", [P, 9728])
    rnd = sb("rnd", [P, 4 * KT * T], F32R)

    free = [0]

    def region(*shape, of=arena):
        n = 1
        for s in shape:
            n *= s
        a = of[:, free[0]:free[0] + n]
        free[0] += n
        assert free[0] <= of.shape[1]
        names = "abcd"[:len(shape)]
        if len(shape) > 1:
            a = a.rearrange(f"p ({' '.join(names)}) -> p {' '.join(names)}", **dict(zip(names, shape)))
        return a

    qT, kT = region(4, T), region(4, T)
    v_tok = region(NG, COLS)
    k_tok = region(COLS)
    conv_u, conv_c = region(4, T), region(4, T)
    kc_tok, vc_tok = region(COLS), region(COLS)
    kcT = region(PAIRS, P)
    bias = region(HEADS, P)
    probs, probsT = region(2, 3 * P), region(2, 3 * P)
    free[0] = 2 * 4 * T + NG * COLS + COLS
    ffn_silu, ffn_prod = region(2, T), region(2, T)
    ffn_end = free[0]
    free[0] = 0
    dftn = region(2, KT, T)
    free[0] = max(free[0], ffn_end)
    dft = region(DFT_N)
    free[0] = 0
    take = region(NG, EXPERTS + 1, SLOTS)
    giveT = region(EXPERTS, T)
    acc = region(KT, T)
    give_at = free[0]
    give = region(NG, EXPERTS, SLOTS)
    free[0] = give_at
    moe_silu, moe_g = region(2, COLS), region(2, COLS)
    y_slot = region(D)
    free[0] = 0
    h_r = [region(KT, T, of=rnd) for _ in range(2)]
    mix_r = [region(KT, T, of=rnd) for _ in range(2)]
    free[0] = 2 * KT * T
    ffn_r = [region(2, 4, T, of=rnd) for _ in range(2)]
    f_r = h_r
    free[0] = 0
    hg_r = [region(KT, SLOTS, of=rnd) for _ in range(2)]
    gt_r = [region(2, 4, SLOTS, of=rnd) for _ in range(2)]

    def C(name):
        a, b = CONST_AT[name]
        return cst[:, a:b]

    def DFT(name):
        a, b = DFT_AT[name]
        return dft[:, a:b]

    ident, ones, mask, earlier = C("ident"), C("ones"), C("mask"), C("earlier")
    diag = C("diag")[0:BIAS_COLS]
    dft_pos = DFT("dft_pos")
    dft_cos = DFT("dft_cos").rearrange("p (a b) -> p a b", a=2)
    dft_sin = DFT("dft_sin").rearrange("p (a b) -> p a b", a=2)
    ada_rows = tok[0:4, 0, :].rearrange("p (i n) -> p i n", i=2)

    neg_max = small[:, 0:4].rearrange("p (a b) -> p a b", a=2)
    row_max = small[:, 4:8].rearrange("p (a b) -> p a b", a=2)
    row_sum = small[:, 8:12].rearrange("p (a b) -> p a b", a=2)
    row_inv = small[:, 12:16].rearrange("p (a b) -> p a b", a=2)
    logits = small[:, 16:32].rearrange("p (g e) -> p g e", g=NG)
    top = small[:, 32:48].rearrange("p (g e) -> p g e", g=NG)
    idx_f = small[:, 48:64].rearrange("p (g e) -> p g e", g=NG)
    gap, gap_exp, gate_den = small[:, 64:66], small[:, 66:68], small[:, 68:70]
    gate_1, gate_2 = small[:, 70:72], small[:, 72:74]
    hot_1 = small[:, 80:96].rearrange("p (g e) -> p g e", g=NG)
    hot_2 = small[:, 96:112].rearrange("p (g e) -> p g e", g=NG)
    chosen = small[:, 112:128].rearrange("p (g e) -> p g e", g=NG)
    gates = small[:, 128:144].rearrange("p (g e) -> p g e", g=NG)
    rank = small[:, 144:160].rearrange("p (g e) -> p g e", g=NG)
    counts = small[:, 160:168]
    most_f = small[:, 168:169]

    ps = ctx.enter_context(nc.psum_tensor("ps", [P, 8, 512], F32))

    raw_full = [sem(f"raw_full{i}") for i in range(RAW)]
    hi_done, lo_done = sem("hi_done"), sem("lo_done")
    part_used = sem("part_used")
    in_vec, in_const, in_x, in_cache, in_small, in_dft = (
        sem(n) for n in ("in_vec", "in_const", "in_x", "in_cache", "in_small", "in_dft"))
    mm_done = sem("mm_done")
    evac_done = sem("evac_done")
    dve_step = sem("dve_step")
    cond_silu, cond_hi, cond_ready = sem("cond_silu"), sem("cond_hi"), sem("cond_ready")
    sq_done = sem("sq_done")
    std_ready = sem("std_ready")
    h_scaled = sem("h_scaled")
    h_ready = sem("h_ready")
    h_rest = sem("h_rest")
    sc_full, sc_free, mx_ready, exp_done = sem("sc_full"), sem("sc_free"), sem("mx_ready"), sem("exp_done")
    p_ready, pt_full, pt_copied, pv_done = sem("p_ready"), sem("pt_full"), sem("pt_copied"), sem("pv_done")
    up_done, silu_done, g_done, down_done = sem("up_done"), sem("silu_done"), sem("g_done"), sem("down_done")
    ffn_added = sem("ffn_added")
    chosen_ready = sem("chosen_ready")
    gap_ready, gap_exp_done = sem("gap_ready"), sem("gap_exp_done")
    acc_zero = sem("acc_zero")
    most_ready = sem("most_ready")
    rank_moved = sem("rank_moved")
    take_built = sem("take_built")
    give_full, give_copied = sem("give_full"), sem("give_copied")
    hg_full, hg_hi, hg_lo = sem("hg_full"), sem("hg_hi"), sem("hg_lo")
    e_used = sem("e_used")
    e_silu, e_g = sem("e_silu"), sem("e_g")
    e_turned, gt_hi, gt_lo = sem("e_turned"), sem("gt_hi"), sem("gt_lo")
    y_out = sem("y_out")
    e_spread = sem("e_spread")
    acc_added = sem("acc_added")
    moe_added = sem("moe_added")
    y_ready = sem("y_ready")
    out_kv, out_y = sem("out_kv"), sem("out_y")
    CREDIT = STAGE

    def half_view(buf, slot, h):
        name, rows, cols = h
        r, n = (rows.stop - rows.start) // P, cols.stop - cols.start
        return buf[:, slot, 0:r * n].rearrange("p (k n) -> p k n", n=n)

    def moe_half(name, s, half):
        if name == "w2":
            return name, slice(s * COLS + half * 256, s * COLS + half * 256 + 256), slice(0, D)
        return name, slice(half * D // 2, (half + 1) * D // 2), slice(s * COLS, (s + 1) * COLS)

    used_up = []
    at_turn = {}
    halves_at = {}
    turn_half = []
    att_half = []
    up_half = []
    norm_turn = []

    def ada_order(units):
        order = []
        for n, u in enumerate(units):
            order.append(("rows", u, n % 2))
            if n:
                order.append(("cols", units[n - 1], (n - 1) % 2))
        return order + [("cols", units[-1], (len(units) - 1) % 2)]

    signal_of_turn = {}

    def turn_half_of(n):
        return turn_half[signal_of_turn[n]]

    def norm_half(k):
        return turn_half_of(norm_turn[k] - 1)

    def ffn_cols(s):
        return min(COLS, FFN - s * COLS)

    block = ctx.enter_context(nc.Block())

    @block.tensor
    def _(pe):
        turn = [0]
        signals = [0]
        parts = [0]
        half_n = [0]

        def done(last):
            signal_of_turn[turn[0] - 1] = signals[0]
            signals[0] += 1
            turn_half.append(half_n[0])
            last.then_inc(mm_done, 1)

        def bank():
            n = turn[0]
            if n >= ROT:
                pe.wait_ge(evac_done, n - ROT + 1)
            turn[0] += 1
            return ps[:, n % ROT, :]

        def weights(name):
            n = half_n[0]
            half_n[0] += 1
            assert PLAN[n][0] == name, (n, PLAN[n], name)
            pe.wait_ge(lo_done, n + 1)
            return half_view(w_hi, n % STAGE, PLAN[n]), half_view(w_lo, n % STAGE, PLAN[n])

        def used_in_part(last):
            parts[0] += 1
            last.then_inc(part_used, 1)
            used_up.append((part_used, parts[0]))

        def mm(out, lhsT, rhs, first, last, **kw):
            return pe.matmul(out, lhsT, rhs, start=first, stop=last, **kw)

        def mm3(out, a, b, first, last, **kw):
            mm(out, a[0], b[0], first, False, **kw)
            mm(out, a[0], b[1], False, False, **kw)
            return mm(out, a[1], b[0], False, last, **kw)

        def transposes(srcs):
            b = bank()
            for i, s in enumerate(srcs):
                n = s.shape[0]
                last = pe.transpose(b[0:s.shape[1], i * n:(i + 1) * n], s, ident[0:n, 0:n])
            done(last)

        def ada(l, units):
            for what, u, i in ada_order(units):
                b = bank()
                if what == "rows":
                    for part in range(2):
                        w = weights(f"ada{l}")
                        for k in range(4):
                            c = cond_r[:, 4 * (4 * part + k):4 * (4 * part + k) + P]
                            first, end = part == 0 and k == 0, part == 1 and k == 3
                            mm(b, c, w[0][:, k, :], first, False)
                            last = mm(b, c, w[1][:, k, :], False, end)
                        if part == 0:
                            used_in_part(last)
                    done(last)
                    used_up.append((mm_done, signals[0]))
                else:
                    pe.wait_ge(evac_done, turn[0] - 2 if (what, u) != ("cols", units[-1]) else turn[0] - 1)
                    for j in range(4):
                        last = mm(b[:, NG * j:NG * j + NG], ada_rows[:, i, j * P:(j + 1) * P], C("pair_sum")[0:4], True,
                                  True)
                    done(last)

        def project(name, src, chunk_hook=None, chunk_ready=None):
            for part in range(2):
                w = weights(name)
                for j in range(2):
                    b = bank()
                    for k in range(KT):
                        if chunk_ready and part == 0 and j == 0:
                            chunk_ready(k)
                        sl = slice(j * P, (j + 1) * P)
                        last = mm3(b[:, 0:T], (w[0][:, k, sl], w[1][:, k, sl]), (src[0][:, k, :], src[1][:, k, :]),
                                   k == 0, k == KT - 1)
                    done(last)
                    if j == 1:
                        used_up.append((mm_done, signals[0]))
                    if chunk_hook:
                        chunk_hook()

        def norm_sum(k):
            b = bank()
            for c in range(KT):
                pe.wait_ge(sq_done, KT * k + c + 1)
                last = mm(b[:, 0:T], ones, hT[:, c, :], c == 0, c == KT - 1)
            done(last)
            norm_turn.append(turn[0])

        def h_tokens():
            for g in range(NG):
                for half in range(2):
                    transposes([hT[:, 4 * half + i, g * P:(g + 1) * P] for i in range(4)])

        pe.wait_ge(in_const, 16)
        pe.wait_ge(in_vec, 16 * 7)
        transposes([vec_rows[0:36, 1, :]])
        transposes([vec_rows[:, 0, :]])
        pe.wait_ge(in_x, 32)
        for g in range(NG):
            for half in range(2):
                transposes([tok[:, g, (4 * half + i) * P:(4 * half + i + 1) * P] for i in range(4)])
        at_turn["x"] = turn[0]
        norm_sum(0)
        pe.wait_ge(in_cache, 32)
        transposes([kc_tok[:, i * P:(i + 1) * P] for i in range(4)])
        pe.wait_ge(in_small, 16 * (HEADS + 2))
        transposes([rpb_rows[:]])
        pe.wait_ge(evac_done, turn[0])
        for q in range(4):
            b = bank()
            for i in range(16):
                kc = 16 * q + i
                last = mm(b[0:GRID_W, 24 * i:24 * (i + 1)], diag[:, GRID_W - 1 - kc:2 * GRID_W - 1 - kc], rpbT[:],
                          True, True)
            done(last)
        pe.wait_ge(cond_ready, 1)
        ada(0, range(4))

        def h_chunk(k):
            pe.wait_ge(h_rest, NG * (k + 1))

        halves_at["q"] = half_n[0]
        project("win", h_r, chunk_ready=h_chunk)
        project("win", h_r)
        halves_at["v"] = half_n[0]
        banks = [bank(), bank()]
        for part in range(2):
            w = weights("win")
            for g in range(NG):
                for k in range(4):
                    kt = 4 * part + k
                    sl = slice(g * P, (g + 1) * P)
                    last = mm3(banks[g], (h_r[0][:, kt, sl], h_r[1][:, kt, sl]), (w[0][:, k, :], w[1][:, k, :]),
                               kt == 0, kt == KT - 1)
                if part:
                    done(last)
            if part == 0:
                used_in_part(last)
        used_up.append((mm_done, signals[0]))
        pe.wait_ge(evac_done, turn[0] - 2)
        transposes([kT[:, c, 0:P] for c in range(4)])

        def scores(h):
            if h >= 2:
                pe.wait_ge(sc_free, h - 1)
            b, o, c = ps[:, 4 + h % 2, :], HD * (h % 2), h // 2
            for g in range(NG):
                mm(b[:, g * P:(g + 1) * P], qT[o:o + HD, c, g * P:(g + 1) * P], kT[o:o + HD, c, g * P:(g + 1) * P],
                   True, True)
            mm(b[:, 2 * P:3 * P], qT[o:o + HD, c, P:T], kcT[o:o + HD, c, :], True, True).then_inc(sc_full, 1)

        def turn_probs(h):
            pe.wait_ge(p_ready, h + 1)
            if h >= 2:
                pe.wait_ge(pt_copied, h - 1)
            for i in range(3):
                last = pe.transpose(ps[:, 6 + h % 2, i * P:(i + 1) * P], probs[:, h % 2, i * P:(i + 1) * P], ident)
            last.then_inc(pt_full, 1)

        def values(h, b):
            pe.wait_ge(pt_copied, h + 1)
            o, c = HD * (h % 2), HD * h
            pt = probsT[:, h % 2, :]
            mm(b[o:o + HD, 0:P], v_tok[:, 0, c:c + HD], pt[:, 0:P], True, True)
            mm(b[o:o + HD, P:T], v_tok[:, 1, c:c + HD], pt[:, P:T], True, False)
            last = mm(b[o:o + HD, P:T], vc_tok[:, c:c + HD], pt[:, T:T + P], False, True)
            last.then_inc(pv_done, 1)

        step = [0]

        def attention_step():
            i = step[0]
            step[0] += 1
            att_half.append(half_n[0])
            if i < HEADS:
                scores(i)
            if 2 <= i < HEADS + 2:
                turn_probs(i - 2)
            if 3 <= i < HEADS + 3 and (i - 3) % 2:
                b = bank()
                values(i - 4, b)
                values(i - 3, b)

        at_turn["cache"] = turn[0]
        for _u in range(3):
            project("win", h_r, attention_step)
        ada(0, (4, 5))
        pe.wait_ge(evac_done, turn[0] - 2)
        at_turn["wout"] = turn[0]
        halves_at["wout"] = half_n[0]
        for _u in range(2):
            project("wout", mix_r)
        ada(0, range(6, 10))
        norm_sum(1)
        ada(0, (10, 11))
        halves_at["ffn"] = half_n[0]

        ups, downs = [0], [0]

        def up(s):
            for c in range(0, ffn_cols(s), COLS // 2):
                banks_ = [4 + (ups[0] + i) % 4 for i in range(2)]
                for n, name in enumerate(("w1", "w3")):
                    w = weights(name)
                    for i in range(2):
                        if n == 0 and ups[0] + i >= 4:
                            pe.wait_ge(g_done, ups[0] + i - 3)
                        for k in range(KT):
                            if s == 0 and c == 0 and n == 0 and i == 0:
                                pe.wait_ge(h_rest, NG * (KT + k + 1))
                            sl = slice(i * P, (i + 1) * P)
                            last = mm3(ps[:, banks_[i], n * T:(n + 1) * T], (w[0][:, k, sl], w[1][:, k, sl]),
                                       (h_r[0][:, k, :], h_r[1][:, k, :]), k == 0, k == KT - 1)
                        if n:
                            last.then_inc(up_done, 1)
                            up_half.append(half_n[0])
                    if n:
                        used_up.append((up_done, ups[0] + 2))
                    else:
                        used_in_part(last)
                ups[0] += 2

        def down(s):
            for part in range(ffn_cols(s) * 2 // COLS):
                w = weights("w2")
                for i in range(2):
                    f = 2 * part + i
                    pe.wait_ge(g_done, 4 * s + f + 1)
                    for o in range(KT):
                        sl = slice(o * P, (o + 1) * P)
                        last = mm3(ps[:, o // 2, (o % 2) * T:(o % 2 + 1) * T], (w[0][:, i, sl], w[1][:, i, sl]),
                                   (ffn_r[0][:, s % 2, f, :], ffn_r[1][:, s % 2, f, :]),
                                   s == 0 and f == 0 and o % 2 == 0, 4 * s + f == FFN // P - 1, skip_group_check=True)
                last.then_inc(down_done, 1)
                downs[0] += 1
                used_up.append((down_done, downs[0]))

        before_ffn = turn[0]
        up(0)
        for s in range(1, FFN_SLICES):
            up(s)
            if s == 1:
                pe.wait_ge(evac_done, before_ffn)
            down(s - 1)
        down(FFN_SLICES - 1)
        halves_at["ffn_end"] = half_n[0]

        pe.wait_ge(ffn_added, KT)
        ada(1, range(4))
        norm_sum(2)
        ada(1, (4, 5))
        halves_at["fourier"] = half_n[0]
        pe.wait_ge(h_ready, 48)
        h_tokens()
        pe.wait_ge(evac_done, turn[0])
        pe.wait_ge(in_dft, 16)
        for g in range(NG):
            for cp in range(4):
                b = bank()
                for i in range(2):
                    c = 2 * cp + i
                    last = mm(b[:, i * T:(i + 1) * T], tok[:, g, c * P:(c + 1) * P], dft_pos, True, True)
                done(last)
        pe.wait_ge(evac_done, turn[0])
        for o in range(KT):
            grp, oc = o // 2, o % 2
            b = bank()
            for n, mat in enumerate((dft_cos, dft_sin)):
                for ic in range(2):
                    last = mm(b[:, 0:T], mat[:, ic, oc * P:(oc + 1) * P], dftn[:, n, 2 * grp + ic, :],
                              n == 0 and ic == 0, n == 1 and ic == 1)
            done(last)
        pe.wait_ge(evac_done, turn[0])
        at_turn["wf"] = turn[0]
        for _u in range(2):
            project("wf", f_r)
        ada(1, range(6, 10))
        norm_sum(3)
        ada(1, (10, 11))
        halves_at["router"] = half_n[0]

        pe.wait_ge(h_ready, 64)
        b = bank()
        for g in range(NG):
            for k in range(KT):
                last = mm(b[:, EXPERTS * g:EXPERTS * (g + 1)], hT[:, k, g * P:(g + 1) * P], router[:, k, :],
                          k == 0, k == KT - 1)
        done(last)
        h_tokens()
        pe.wait_ge(chosen_ready, 1)
        b = bank()
        mm(b[:, 0:8], earlier, chosen[:, 0, :], True, True)
        mm(b[:, 8:16], earlier, chosen[:, 1, :], True, False)
        mm(b[:, 8:16], ones, chosen[:, 0, :], False, True)
        mm(b[:, 16:24], ones, chosen[:, 0, :], True, False).then_inc(e_used, CREDIT)
        done(mm(b[:, 16:24], ones, chosen[:, 1, :], False, True))
        pe.wait_ge(evac_done, turn[0])

        def turn_give(r):
            pe.wait_ge(take_built, r + 1)
            for q in range(4):
                for i in range(4):
                    e, g = 2 * q + i // 2, i % 2
                    last = pe.transpose(ps[0:SLOTS, q, i * P:(i + 1) * P], give[:, g, e, :], ident)
                last.then_inc(give_full, 1)
            pe.wait_ge(give_copied, 4 * r + 4)

        def gather(e, banks_ready):
            for q in range(2):
                b = ps[:, 6 + q, :]
                if q == 1:
                    banks_ready()
                for i in range(4):
                    c = 4 * q + i
                    for g in range(NG):
                        last = mm(b[:, i * SLOTS:(i + 1) * SLOTS], tok[:, g, c * P:(c + 1) * P],
                                  take[:, g, bass.ds(e, 1), :].rearrange("p o s -> p (o s)"), g == 0, g == NG - 1)
                last.then_inc(hg_full, 1)

        def expert(job, e, r):
            at = [0]

            def half():
                i = at[0]
                at[0] += 1
                slot = (N_PRE + i) % STAGE
                pe.wait_ge(lo_done, N_PRE + i + 1 + MOE_HALVES * job)
                h = moe_half(*MOE_PLAN[i])
                return half_view(w_hi, slot, h), half_view(w_lo, slot, h)

            def up(s, n):
                b = ps[:, 2 + 2 * (s % 2) + n, :]
                for part in range(2):
                    w = half()
                    for k in range(4):
                        kt = 4 * part + k
                        last = mm3(b, (hg_r[0][:, kt, :], hg_r[1][:, kt, :]), (w[0][:, k, :], w[1][:, k, :]),
                                   kt == 0, kt == KT - 1)
                    last.then_inc(e_used, 1)

            def turn_g(s):
                pe.wait_ge(e_g, MOE_SLICES * job + s + 1)
                b = ps[:, 6 + s % 2, :]
                for i in range(4):
                    last = pe.transpose(b[:, i * SLOTS:(i + 1) * SLOTS], moe_g[:, s % 2, i * P:(i + 1) * P], ident)
                last.then_inc(e_turned, 1)

            def down(s, part):
                w = half()
                pe.wait_ge(gt_lo, MOE_SLICES * job + s + 1)
                for i in range(2):
                    f = 2 * part + i
                    for o in range(2):
                        sl = slice(o * COLS, (o + 1) * COLS)
                        last = mm3(ps[:, o, :], (gt_r[0][:, s % 2, f, :], gt_r[1][:, s % 2, f, :]),
                                   (w[0][:, i, sl], w[1][:, i, sl]), s == 0 and f == 0,
                                   s == MOE_SLICES - 1 and f == 3)
                last.then_inc(e_used, 1)

            pe.wait_ge(hg_lo, 2 * (job + r + 1))
            for s in range(MOE_SLICES):
                if s == 0:
                    pe.wait_ge(acc_added, 4 * job - 2 + CREDIT)
                elif s == 1:
                    pe.wait_ge(acc_added, 4 * job + CREDIT)
                else:
                    pe.wait_ge(e_g, MOE_SLICES * job + s - 1)
                up(s, 0)
                if s:
                    turn_g(s - 1)
                up(s, 1)
                if 0 < s < MOE_SLICES - 1:
                    down(s - 1, 0)
                    down(s - 1, 1)
            gather(e + 1, lambda: pe.wait_ge(gt_lo, MOE_SLICES * job + MOE_SLICES - 1))
            down(MOE_SLICES - 2, 0)
            pe.wait_ge(hg_lo, 2 * (job + r + 1) + 1)
            turn_g(MOE_SLICES - 1)
            down(MOE_SLICES - 2, 1)
            down(MOE_SLICES - 1, 0)
            down(MOE_SLICES - 1, 1)
            for q in range(4):
                if q % 2 == 0:
                    pe.wait_ge(y_out, 2 * job + q // 2 + 1)
                for i in range(2):
                    c = 2 * q + i
                    last = mm(ps[:, 2 + q, i * T:(i + 1) * T], y_slot[:, c * P:(c + 1) * P],
                              giveT[:, bass.ds(e, 1), :].rearrange("p o t -> p (o t)"), True, True)
                last.then_inc(e_spread, 1)

        turn_give(0)
        gather(0, lambda: None)
        with pe.Fori(0, EXPERTS) as e:
            expert(e, e, 0)
        most_here = pe.value_load(most[0:1, 0:1], min_val=0, max_val=T)
        with pe.If(most_here > SLOTS):
            turn_give(1)
            gather(0, lambda: None)
            with pe.Fori(0, EXPERTS) as e:
                expert(e + EXPERTS, e, 1)
        norm_sum(4)
        pe.wait_ge(y_ready, 16)
        at_turn["out"] = turn[0]
        h_tokens()

    @block.sync
    def _(sp):
        dense = {"ada0": ins["ada_w"][0], "ada1": ins["ada_w"][1], "win": ins["w_in"][0], "wout": ins["w_out"][0],
                 "wf": ins["fourier_w"][0], "w1": ins["ffn_w1"][0], "w3": ins["ffn_w3"][0], "w2": ins["ffn_w2"][0]}
        vec_loads = [(0, 1, KT, ins["c_ctx"].rearrange("(k p) -> k p", p=P)),
                     (8, 1, KT, ins["c"][0].rearrange("(k p) -> k p", p=P)),
                     (16, 1, KT, ins["final_g"].rearrange("(k p) -> k p", p=P)),
                     (24, 1, 12, ins["conv_w"][0].rearrange("j (k p) -> (j k) p", p=P)),
                     (0, 0, 96, ins["ada_b"].rearrange("l (k p) -> (l k) p", p=P)),
                     (96, 0, 16, ins["norm1_g"].rearrange("l (k p) -> (l k) p", p=P)),
                     (112, 0, 16, ins["norm2_g"].rearrange("l (k p) -> (l k) p", p=P))]
        for at, tile, n, src in vec_loads:
            sp.dma_start(vec_rows[at:at + n, tile, :], src).then_inc(in_vec, 16)
        sp.dma_start(cst[:], consts).then_inc(in_const, 16)
        for n, (name, rows, cols) in enumerate(PLAN):
            if n == 2:
                sp.dma_start(tok[:, 0, :], ins["x_prompt"][0]).then_inc(in_x, 16)
                sp.dma_start(tok[:, 1, :], ins["x_sample"][0]).then_inc(in_x, 16)
            if n >= RAW:
                sp.wait_ge(lo_done, n - RAW + 1)
            sp.dma_start(half_view(raw, n % RAW, PLAN[n]),
                         dense[name][rows, cols].rearrange("(k p) n -> p k n", p=P)).then_inc(raw_full[n % RAW], 16)

        def load_expert(job, e):
            for i, h in enumerate(MOE_PLAN):
                name, rows, cols = moe_half(*h)
                slot = (N_PRE + i) % RAW
                sp.wait_ge(lo_done, N_PRE + i - RAW + 1 + MOE_HALVES * job)
                src = ins["moe_" + name][0, bass.ds(e, 1), rows, cols].rearrange("o (k p) n -> p (o k) n", p=P)
                sp.dma_start(half_view(raw, slot, (name, rows, cols)), src).then_inc(raw_full[slot], 16)

        with sp.Fori(0, EXPERTS) as e:
            load_expert(e, e)
        sp.wait_ge(most_ready, 1)
        most_here = sp.value_load(most[0:1, 0:1], min_val=0, max_val=T)
        with sp.If(most_here > SLOTS):
            with sp.Fori(0, EXPERTS) as e:
                load_expert(e + EXPERTS, e)
        for g, out in enumerate((outs[0], outs[1])):
            sp.wait_ge(evac_done, at_turn["out"] + 2 * g + 2)
            sp.dma_start(out[0], tok[:, g, :]).then_inc(out_y, 16)
        sp.wait_ge(out_y, 32)

    @block.gpsimd
    def _(pool):
        pool.wait_ge(evac_done, at_turn["cache"])
        for n, src in ((2, k_tok), (3, v_tok[:, 0, :])):
            pool.dma_start(outs[n][0, 0].rearrange("h s d -> s h d"),
                           src.rearrange("s (h d) -> s h d", h=HEADS)).then_inc(out_kv, 16)
        pool.wait_ge(out_kv, 32)
        pool.wait_ge(evac_done, at_turn["wout"])
        pool.dma_start(dft, dft_consts).then_inc(in_dft, 16)
        pool.wait_ge(in_dft, 16)
        pool.wait_ge(most_ready, 1)
        pool.memset(acc, 0.0).then_inc(acc_zero, 1)
        pool.memset(take[:, :, EXPERTS, :], 0.0).then_inc(acc_zero, 1)

    @block.scalar
    def _(act):
        act.dma_start(kc_tok.rearrange("l (h d) -> l h d", h=HEADS),
                      ins["cache_k"][0, 0].rearrange("h l d -> l h d")).then_inc(in_cache, 16)
        act.dma_start(vc_tok.rearrange("l (h d) -> l h d", h=HEADS),
                      ins["cache_v"][0, 0].rearrange("h l d -> l h d")).then_inc(in_cache, 16)
        for h in range(HEADS):
            act.dma_start(rpb_rows[BIAS_ROWS * h:BIAS_ROWS * (h + 1), :],
                          ins["rpb"][0, h, WIN_ROWS - 2:WIN_ROWS + 1, :]).then_inc(in_small, 16)
        act.dma_start(router[:], ins["router_w"][0].rearrange("(k p) e -> p k e", p=P)).then_inc(in_small, 16)
        act.dma_start(router_bias[:], ins["router_b"][0:1, :].to_broadcast([P, EXPERTS])).then_inc(in_small, 16)

        split = [0]

        def split_ahead(used):
            while split[0] < min(used + AHEAD, N_PRE):
                n = split[0]
                split[0] += 1
                act.wait_ge(raw_full[n % RAW], 16 * (n // RAW + 1))
                if n >= STAGE:
                    act.wait_ge(*used_up[n - STAGE])
                act.activation(half_view(w_hi, n % STAGE, PLAN[n]), half_view(raw, n % RAW, PLAN[n]),
                               ACT.Copy).then_inc(hi_done, 1)

        act.wait_ge(evac_done, 1)
        act.activation(cond[:].rearrange("p k v -> p v k"), vecB[:, 0:16].rearrange("p (v k) -> p v k", v=NG),
                       ACT.Silu).then_inc(cond_silu, 1)
        act.wait_ge(cond_silu, 1)
        act.wait_ge(cond_hi, 1)
        act.activation(cond_r[:, 0:4 * KT].rearrange("p (k v) -> p k v", v=4)[:, :, 0:2], cond[:],
                       ACT.Copy).then_inc(cond_silu, 1)

        def norm(k, ready, first, used, meanwhile=None):
            for c in range(KT):
                act.wait_ge(ready, first(c))
                act.activation(hT[:, c, :], xT[:, c, :], ACT.Square).then_inc(sq_done, 1)
            split_ahead(used)
            act.wait_ge(evac_done, norm_turn[k])
            act.activation(var[:], var[:], ACT.Sqrt).then_inc(std_ready, 1)
            if k == 0:
                split_ahead(halves_at["q"])
            if k < 4:
                l, half = k // 2, k % 2
                for c in range(KT):
                    for g in range(NG):
                        act.wait_ge(h_scaled, 16 * k + NG * c + g + 1)
                        sl = slice(g * P, (g + 1) * P)
                        dst = h_r[0][:, c, sl] if k < 2 else hT[:, c, sl]
                        act.activation(dst, hT[:, c, sl], ACT.Identity,
                                       bias=mods[:, l, 24 * half + c, g:g + 1]).then_inc(h_ready, 1)

        norm(0, evac_done, lambda c: at_turn["x"], 0)
        for i in range(12):
            split_ahead(att_half[i])
            if i < HEADS:
                act.wait_ge(mx_ready, i + 1)
                act.activation(probs[:, i % 2, 0:P], probs[:, i % 2, 0:P], ACT.Exp, bias=neg_max[:, i % 2, 0:1],
                               accum_out=row_sum[:, i % 2, 0:1])
                act.activation(probs[:, i % 2, P:3 * P], probs[:, i % 2, P:3 * P], ACT.Exp,
                               bias=neg_max[:, i % 2, 1:2], accum_out=row_sum[:, i % 2, 1:2]).then_inc(exp_done, 1)
            if 2 <= i < HEADS + 2:
                h = i - 2
                act.wait_ge(pt_full, h + 1)
                if h >= 2:
                    act.wait_ge(pv_done, h - 1)
                act.activation(probsT[:, h % 2, :], ps[:, 6 + h % 2, 0:3 * P], ACT.Copy).then_inc(pt_copied, 1)
        split_ahead(halves_at["wout"])

        def wout_chunk(c):
            split_ahead(turn_half_of(at_turn["wout"] + c))
            return at_turn["wout"] + c + 1

        def wf_chunk(c):
            split_ahead(turn_half_of(at_turn["wf"] + c))
            return at_turn["wf"] + c + 1

        def ffn_chunk(c):
            split_ahead(halves_at["ffn_end"])
            return c + 1

        norm(1, evac_done, wout_chunk, norm_half(1))
        act.wait_ge(out_kv, 32)
        for a in range(FFN // P):
            split_ahead(up_half[a])
            act.wait_ge(up_done, a + 1)
            if a >= 2:
                act.wait_ge(g_done, a - 1)
            act.activation(ffn_silu[:, a % 2, :], ps[:, 4 + a % 4, 0:T], ACT.Silu).then_inc(silu_done, 1)
        norm(2, ffn_added, ffn_chunk, norm_half(2))
        norm(3, evac_done, wf_chunk, norm_half(3))
        split_ahead(N_PRE)
        act.wait_ge(gap_ready, 1)
        act.activation(gap_exp, gap, ACT.Exp).then_inc(gap_exp_done, 1)

        def hg_round(job, r, q):
            act.wait_ge(hg_full, 2 * (job + r) + q + 1)
            act.activation(hg_r[0][:, 4 * q:4 * q + 4, :], ps[:, 6 + q, :].rearrange("p (c s) -> p c s", c=4),
                           ACT.Copy).then_inc(hg_hi, 1)

        def expert(job, r):
            at = [0]

            def split_to(n):
                while at[0] < n:
                    i = at[0]
                    at[0] += 1
                    slot, m = (N_PRE + i) % STAGE, N_PRE + i
                    act.wait_ge(raw_full[m % RAW], 16 * (m // RAW + 1) + 16 * (MOE_HALVES // RAW) * job)
                    act.wait_ge(e_used, MOE_HALVES * job + i - STAGE + 1 + CREDIT)
                    act.activation(w_hi[:, slot, :], raw[:, m % RAW, :], ACT.Copy).then_inc(hi_done, 1)

            def silu(s):
                act.wait_ge(e_used, MOE_HALVES * job + MOE_PLAN.index(("w1", s, 1)) + 1 + CREDIT)
                act.activation(moe_silu[:, s % 2, :], ps[:, 2 + 2 * (s % 2), :], ACT.Silu).then_inc(e_silu, 1)

            def gt_round(s):
                act.wait_ge(e_turned, MOE_SLICES * job + s + 1)
                act.activation(gt_r[0][:, s % 2, :, :], ps[:, 6 + s % 2, :].rearrange("p (f s) -> p f s", f=4),
                               ACT.Copy).then_inc(gt_hi, 1)

            split_to(4)
            silu(0)
            split_to(6)
            for s in range(1, MOE_SLICES):
                base = MOE_PLAN.index(("w1", s, 0))
                split_to(base + 4)
                silu(s)
                gt_round(s - 1)
                split_to(base + 6)
            hg_round(job + 1, r, 0)
            hg_round(job + 1, r, 1)
            split_to(MOE_HALVES - 1)
            gt_round(MOE_SLICES - 1)
            split_to(MOE_HALVES)
            act.wait_ge(e_used, MOE_HALVES * job + MOE_HALVES + CREDIT)
            for o in range(2):
                act.activation(y_slot[:, o * COLS:(o + 1) * COLS], ps[:, o, :], ACT.Copy).then_inc(y_out, 1)

        for q in range(2):
            hg_round(0, 0, q)
        with act.Fori(0, EXPERTS) as e:
            expert(e, 0)
        most_here = act.value_load(most[0:1, 0:1], min_val=0, max_val=T)
        with act.If(most_here > SLOTS):
            for q in range(2):
                hg_round(EXPERTS, 1, q)
            with act.Fori(0, EXPERTS) as e:
                expert(e + EXPERTS, 1)
        norm(4, moe_added, lambda c: c + 1, N_PRE)

    @block.vector
    def _(dve):
        turn = [0]
        signals = [0]
        steps = [0]
        split = [0]

        def split_ahead(used):
            while split[0] < min(used + AHEAD, N_PRE):
                n = split[0]
                split[0] += 1
                dve.wait_ge(hi_done, n + 1)
                dve.tensor_tensor(half_view(w_lo, n % STAGE, PLAN[n]), half_view(raw, n % RAW, PLAN[n]),
                                  half_view(w_hi, n % STAGE, PLAN[n]).bitcast(F32), ALU.subtract).then_inc(lo_done, 1)

        def full(heads=None):
            n = turn[0]
            turn[0] += 1
            if heads is None:
                if turn_half[signals[0]]:
                    split_ahead(turn_half[signals[0]])
                signals[0] += 1
                dve.wait_ge(mm_done, signals[0])
            else:
                dve.wait_ge(pv_done, heads)
            return ps[:, n % ROT, :]

        def link(ins_):
            steps[0] += 1
            ins_.then_inc(dve_step, 1)
            dve.wait_ge(dve_step, steps[0])

        def copy_turn(dst, view):
            b = full()
            dve.tensor_copy(dst, view(b)).then_inc(evac_done, 1)

        def split_turn(dst, b):
            link(dve.tensor_copy(dst[0], b))
            dve.tensor_tensor(dst[1], b, dst[0].bitcast(F32), ALU.subtract).then_inc(evac_done, 1)

        def mod(l, part):
            return mods[:, l, 8 * part:8 * part + 8, :]

        def ada(l, units):
            for what, u, i in ada_order(units):
                b = full()
                if what == "rows":
                    dve.tensor_copy(ada_rows[:, i, :], b[0:4, :]).then_inc(evac_done, 1)
                else:
                    bias_ = vecA[:, 48 * l + 4 * u:48 * l + 4 * u + 4]
                    bias_ = bias_.rearrange("p (c o) -> p c o", o=1).to_broadcast([P, 4, NG])
                    dve.tensor_tensor(mods[:, l, 4 * u:4 * u + 4, :], b[:, 0:8].rearrange("p (c v) -> p c v", c=4),
                                      bias_, ALU.add).then_inc(evac_done, 1)

        def coefs(k):
            l, half = k // 2, k % 2
            g = vecA[:, 96 + 16 * half + 8 * l:96 + 16 * half + 8 * l + 8]
            dve.wait_ge(evac_done, turn[0])
            link(dve.scalar_tensor_tensor(coef[:, k, :, :], mod(l, 3 * half + 1), 1.0,
                                          g.rearrange("p (c o) -> p c o", o=1).to_broadcast([P, KT, NG]),
                                          ALU.add, ALU.mult))

        def mean_square():
            b = full()
            dve.tensor_scalar(var[:], b[:, 0:T], 1.0 / D, EPS, ALU.mult, ALU.add).then_inc(evac_done, 1)

        def scale_rows(k):
            dve.wait_ge(std_ready, k + 1)
            link(dve.reciprocal(rstd[:], var[:]))
            lag = 2
            for c in range(KT + lag):
                for g in range(NG):
                    sl = slice(g * P, (g + 1) * P)
                    if c < KT:
                        scalar = coef[:, k, c, g:g + 1] if k < 4 else vecB[:, 16 + c:17 + c]
                        dve.scalar_tensor_tensor(hT[:, c, sl], xT[:, c, sl], scalar, rstd[:, sl], ALU.mult,
                                                 ALU.mult).then_inc(h_scaled if k < 4 else y_ready, 1)
                    if k < 2 and c >= lag:
                        d = c - lag
                        dve.wait_ge(h_ready, 16 * k + NG * d + g + 1)
                        dve.scalar_tensor_tensor(h_r[1][:, d, sl], hT[:, d, sl], mods[:, 0, 24 * k + d, g:g + 1],
                                                 h_r[0][:, d, sl].bitcast(F32), ALU.add, ALU.subtract).then_inc(h_rest, 1)

        def residual(l, part):
            for c in range(KT):
                b = full()
                for g in range(NG):
                    sl = slice(g * P, (g + 1) * P)
                    last = dve.scalar_tensor_tensor(xT[:, c, sl], b[:, sl], mods[:, l, 8 * part + c, g:g + 1],
                                                    xT[:, c, sl], ALU.mult, ALU.add)
                last.then_inc(evac_done, 1)

        def h_tokens():
            for g in range(NG):
                for half in range(2):
                    copy_turn(tok[:, g, half * COLS:(half + 1) * COLS], lambda b: b)

        dve.memset(cond_r[:].bitcast(F32), 0.0).then_inc(cond_hi, 1)
        copy_turn(vecB[:], lambda b: b[:, 0:36])
        copy_turn(vecA[:], lambda b: b[:, 0:P])
        for g in range(NG):
            for half in range(2):
                copy_turn(xT[:, 4 * half:4 * half + 4, g * P:(g + 1) * P],
                          lambda b: b.rearrange("p (c t) -> p c t", c=4))
        dve.wait_ge(cond_silu, 2)
        cond_v = cond_r[:, 0:4 * KT].rearrange("p (k v) -> p k v", v=4)
        dve.tensor_tensor(cond_v[:, :, 2:4], cond[:], cond_v[:, :, 0:2].bitcast(F32), ALU.subtract).then_inc(cond_ready, 1)
        mean_square()
        split_ahead(0)
        copy_turn(kcT, lambda b: b.rearrange("p (c t) -> p c t", c=4))
        copy_turn(rpbT[:], lambda b: b[0:BIAS_COLS, 0:24])
        for q in range(4):
            b = full()[:, 0:384].rearrange("p (k h r) -> p h k r", h=HEADS, r=BIAS_ROWS)
            for qr in range(GRID_R):
                rows = slice(qr * GRID_W, (qr + 1) * GRID_W)
                for kr in range(GRID_R):
                    cols = slice(kr * GRID_W + 16 * q, kr * GRID_W + 16 * q + 16)
                    m = mask[0:GRID_W, cols].rearrange("p (o k) -> p o k", o=1).to_broadcast([GRID_W, HEADS, 16])
                    last = dve.tensor_tensor(bias[rows, :, cols], b[0:GRID_W, :, :, kr - qr + 1], m, ALU.add)
            last.then_inc(evac_done, 1)
        ada(0, range(4))
        coefs(0)
        scale_rows(0)
        for dst in (qT, kT):
            for c in range(4):
                copy_turn(dst[:, c, :], lambda b: b[:, 0:T])
        for g in range(NG):
            copy_turn(v_tok[:, g, :], lambda b: b)
        copy_turn(k_tok, lambda b: b)

        def soften(h):
            dve.wait_ge(sc_full, h + 1)
            if h >= 2:
                dve.wait_ge(pt_full, h - 1)
            b = ps[:, 4 + h % 2, 0:3 * P].rearrange("p (n t) -> p n t", n=3)
            s = probs[:, h % 2, :].rearrange("p (n t) -> p n t", n=3)
            dve.tensor_scalar(s[:, 0:3:2, :], b[:, 0:3:2, :], SCALE, None, ALU.mult)
            dve.scalar_tensor_tensor(s[:, 1, :], b[:, 1, :], SCALE, bias[:, h, :], ALU.mult, ALU.add).then_inc(sc_free, 1)
            dve.wait_ge(sc_free, h + 1)
            dve.reduce_max(row_max[:, h % 2, 0:1], probs[:, h % 2, 0:P], AX_X)
            link(dve.reduce_max(row_max[:, h % 2, 1:2], probs[:, h % 2, P:3 * P], AX_X))
            dve.tensor_scalar(neg_max[:, h % 2, :], row_max[:, h % 2, :], -1.0, None, ALU.mult).then_inc(mx_ready, 1)

        def normalise(h):
            dve.wait_ge(exp_done, h + 1)
            link(dve.reciprocal(row_inv[:, h % 2, :], row_sum[:, h % 2, :]))
            dve.tensor_scalar(probs[:, h % 2, 0:P], probs[:, h % 2, 0:P], row_inv[:, h % 2, 0:1], None, ALU.mult)
            dve.tensor_scalar(probs[:, h % 2, P:3 * P], probs[:, h % 2, P:3 * P], row_inv[:, h % 2, 1:2], None,
                              ALU.mult).then_inc(p_ready, 1)

        def tap(j, c):
            return vecB[:, 24 + 4 * j + c:25 + 4 * j + c]

        def convolve(c):
            u = conv_u[:, c, :].rearrange("p (g t) -> p g t", g=NG)
            y = conv_c[:, c, :].rearrange("p (g t) -> p g t", g=NG)
            link(dve.tensor_scalar(y, u, tap(1, c), None, ALU.mult))
            link(dve.scalar_tensor_tensor(y[:, :, 1:P], u[:, :, 0:P - 1], tap(0, c), y[:, :, 1:P], ALU.mult, ALU.add))
            link(dve.scalar_tensor_tensor(y[:, :, 0:P - 1], u[:, :, 1:P], tap(2, c), y[:, :, 0:P - 1], ALU.mult, ALU.add))

        for i in range(12):
            b = full()
            part, c = i // 4, i % 4
            if part == 0:
                dve.tensor_copy(conv_c[:, c, :], b[:, 0:T]).then_inc(evac_done, 1)
            elif part == 1:
                dve.tensor_tensor(conv_u[:, c, :], b[:, 0:T], conv_c[:, c, :], ALU.mult).then_inc(evac_done, 1)
            else:
                dve.tensor_tensor(conv_u[:, c, :], b[:, 0:T], conv_c[:, c, :], ALU.mult).then_inc(evac_done, 1)
            if i < HEADS:
                soften(i)
            if 1 <= i < HEADS + 1:
                normalise(i - 1)
            if part == 1:
                dve.wait_ge(evac_done, turn[0])
                convolve(c)
            elif part == 2:
                dve.wait_ge(evac_done, turn[0])
                link(dve.tensor_copy(mix_r[0][:, c, :], conv_u[:, c, :]))
                dve.tensor_tensor(mix_r[1][:, c, :], conv_u[:, c, :], mix_r[0][:, c, :].bitcast(F32), ALU.subtract)
            if 3 <= i < HEADS + 3 and (i - 3) % 2:
                c = 4 + (i - 3) // 2
                split_turn((mix_r[0][:, c, :], mix_r[1][:, c, :]), full(i - 2)[:, 0:T])
        ada(0, (4, 5))
        dve.wait_ge(evac_done, turn[0])
        residual(0, 2)
        ada(0, range(6, 10))
        coefs(1)
        mean_square()
        split_ahead(norm_half(1))
        scale_rows(1)
        ada(0, (10, 11))
        for a in range(FFN // P):
            s, f = a // 4, a % 4
            split_ahead(up_half[a])
            dve.wait_ge(silu_done, a + 1)
            link(dve.tensor_tensor(ffn_prod[:, a % 2, :], ps[:, 4 + a % 4, T:2 * T], ffn_silu[:, a % 2, :], ALU.mult))
            link(dve.tensor_copy(ffn_r[0][:, s % 2, f, :], ffn_prod[:, a % 2, :]))
            dve.tensor_tensor(ffn_r[1][:, s % 2, f, :], ffn_prod[:, a % 2, :], ffn_r[0][:, s % 2, f, :].bitcast(F32),
                              ALU.subtract).then_inc(g_done, 1)
        split_ahead(halves_at["ffn_end"])
        dve.wait_ge(down_done, FFN // (COLS // 2))
        dve.wait_ge(evac_done, turn[0])
        for c in range(KT):
            for g in range(NG):
                sl = slice(g * P, (g + 1) * P)
                off = (c % 2) * T + g * P
                last = dve.scalar_tensor_tensor(xT[:, c, sl], ps[:, c // 2, off:off + P], mods[:, 0, 40 + c, g:g + 1],
                                                xT[:, c, sl], ALU.mult, ALU.add)
            last.then_inc(ffn_added, 1)
        ada(1, range(4))
        coefs(2)
        mean_square()
        split_ahead(norm_half(2))
        scale_rows(2)
        ada(1, (4, 5))
        h_tokens()
        dve.wait_ge(out_kv, 32)
        for g in range(NG):
            for cp in range(4):
                copy_turn(dftn[:, :, 2 * cp:2 * cp + 2, g * P:(g + 1) * P].rearrange("p q c n -> p c q n"),
                          lambda b: b.rearrange("p (c q n) -> p c q n", c=2, q=2))
        for o in range(KT):
            split_turn((f_r[0][:, o, :], f_r[1][:, o, :]), full()[:, 0:T])
        residual(1, 2)
        ada(1, range(6, 10))
        coefs(3)
        mean_square()
        split_ahead(norm_half(3))
        scale_rows(3)
        ada(1, (10, 11))

        b = full()
        dve.tensor_tensor(logits, b[:, 0:16].rearrange("p (g e) -> p g e", g=NG),
                          router_bias[:].rearrange("p (o e) -> p o e", o=1).to_broadcast([P, NG, EXPERTS]),
                          ALU.add).then_inc(evac_done, 1)
        dve.wait_ge(evac_done, turn[0])
        for g in range(NG):
            last = dve.max(top[:, g, :], logits[:, g, :])
        link(last)
        for g in range(NG):
            last = dve.max_index(idx[:, g, :], top[:, g, :], logits[:, g, :])
        link(last)
        dve.tensor_tensor(gap.rearrange("p (g o) -> p g o", o=1), top[:, :, 1:2], top[:, :, 0:1],
                          ALU.subtract).then_inc(gap_ready, 1)
        link(dve.tensor_copy(idx_f, idx[:]))
        for g in range(NG):
            dve.tensor_scalar(hot_1[:, g, :], C("expert_ids"), idx_f[:, g, 0:1], None, ALU.is_equal)
            last = dve.tensor_scalar(hot_2[:, g, :], C("expert_ids"), idx_f[:, g, 1:2], None, ALU.is_equal)
        link(last)
        dve.tensor_tensor(chosen, hot_1, hot_2, ALU.add).then_inc(chosen_ready, 1)
        dve.wait_ge(gap_exp_done, 1)
        link(dve.tensor_scalar(gate_den, gap_exp, 1.0, None, ALU.add))
        link(dve.reciprocal(gate_1, gate_den))
        link(dve.tensor_tensor(gate_2, gate_1, gap_exp, ALU.mult))
        for g in range(NG):
            last = dve.tensor_scalar(gates[:, g, :], hot_1[:, g, :], gate_1[:, g:g + 1], None, ALU.mult)
        link(last)
        for g in range(NG):
            last = dve.scalar_tensor_tensor(gates[:, g, :], hot_2[:, g, :], gate_2[:, g:g + 1], gates[:, g, :],
                                            ALU.mult, ALU.add)
        link(last)
        h_tokens()
        b = full()
        dve.tensor_copy(counts, b[:, 16:24]).then_inc(acc_added, CREDIT)
        dve.tensor_copy(rank, b[:, 0:16].rearrange("p (g e) -> p g e", g=NG)).then_inc(evac_done, 1)
        dve.wait_ge(evac_done, turn[0])
        link(dve.reduce_max(most_f, counts, AX_X))
        dve.tensor_copy(most[:], most_f).then_inc(most_ready, 1)

        def build_round(r):
            if r:
                dve.tensor_scalar(rank, rank, -float(SLOTS), None, ALU.add).then_inc(rank_moved, 1)
                dve.wait_ge(rank_moved, r)
            for g in range(NG):
                for e in range(EXPERTS):
                    dve.tensor_scalar(take[:, g, e, :], C("slot_ids"), rank[:, g, e:e + 1], chosen[:, g, e:e + 1],
                                      ALU.is_equal, ALU.mult)
                    last = dve.tensor_scalar(give[:, g, e, :], C("slot_ids"), rank[:, g, e:e + 1], gates[:, g, e:e + 1],
                                             ALU.is_equal, ALU.mult)
            last.then_inc(take_built, 1)
            for q in range(4):
                dve.wait_ge(give_full, 4 * r + q + 1)
                dve.tensor_copy(giveT[:, 2 * q:2 * q + 2, :],
                                ps[:, q, :].rearrange("p (e t) -> p e t", e=2)).then_inc(give_copied, 1)

        def hg_remainder(job, r, q):
            dve.wait_ge(hg_hi, 2 * (job + r) + q + 1)
            dst = hg_r[1][:, 4 * q:4 * q + 4, :]
            dve.tensor_tensor(dst, ps[:, 6 + q, :].rearrange("p (c s) -> p c s", c=4),
                              hg_r[0][:, 4 * q:4 * q + 4, :].bitcast(F32), ALU.subtract).then_inc(hg_lo, 1)

        def expert(job, r):
            at = [0]

            def split_to(n):
                while at[0] < n:
                    i = at[0]
                    at[0] += 1
                    m, slot = N_PRE + i, (N_PRE + i) % STAGE
                    dve.wait_ge(hi_done, m + 1 + MOE_HALVES * job)
                    dve.tensor_tensor(w_lo[:, slot, :], raw[:, m % RAW, :], w_hi[:, slot, :].bitcast(F32),
                                      ALU.subtract).then_inc(lo_done, 1)

            def gate(s):
                dve.wait_ge(e_silu, MOE_SLICES * job + s + 1)
                dve.wait_ge(e_used, MOE_HALVES * job + MOE_PLAN.index(("w3", s, 1)) + 1 + CREDIT)
                dve.tensor_tensor(moe_g[:, s % 2, :], ps[:, 3 + 2 * (s % 2), :], moe_silu[:, s % 2, :],
                                  ALU.mult).then_inc(e_g, 1)

            def gt_remainder(s):
                dve.wait_ge(gt_hi, MOE_SLICES * job + s + 1)
                dve.tensor_tensor(gt_r[1][:, s % 2, :, :], ps[:, 6 + s % 2, :].rearrange("p (f s) -> p f s", f=4),
                                  gt_r[0][:, s % 2, :, :].bitcast(F32), ALU.subtract).then_inc(gt_lo, 1)

            split_to(6)
            gate(0)
            for s in range(1, MOE_SLICES):
                base = MOE_PLAN.index(("w1", s, 0))
                split_to(base + 4)
                gt_remainder(s - 1)
                split_to(base + 6)
                gate(s)
            hg_remainder(job + 1, r, 0)
            hg_remainder(job + 1, r, 1)
            split_to(MOE_HALVES - 1)
            gt_remainder(MOE_SLICES - 1)
            split_to(MOE_HALVES)
            for q in range(4):
                a = acc[:, 2 * q:2 * q + 2, :]
                dve.wait_ge(e_spread, 4 * job + q + 1)
                dve.tensor_tensor(a, ps[:, 2 + q, :].rearrange("p (c t) -> p c t", c=2), a, ALU.add).then_inc(acc_added, 1)

        dve.wait_ge(acc_zero, 2)
        build_round(0)
        for q in range(2):
            hg_remainder(0, 0, q)
        with dve.Fori(0, EXPERTS) as e:
            expert(e, 0)
        most_here = dve.value_load(most[0:1, 0:1], min_val=0, max_val=T)
        with dve.If(most_here > SLOTS):
            build_round(1)
            for q in range(2):
                hg_remainder(EXPERTS, 1, q)
            with dve.Fori(0, EXPERTS) as e:
                expert(e + EXPERTS, 1)
        dve.wait_ge(acc_added, 4 * EXPERTS + CREDIT)
        for c in range(KT):
            for g in range(NG):
                sl = slice(g * P, (g + 1) * P)
                last = dve.scalar_tensor_tensor(xT[:, c, sl], acc[:, c, sl], mods[:, 1, 40 + c, g:g + 1], xT[:, c, sl],
                                                ALU.mult, ALU.add)
            last.then_inc(moe_added, 1)
        mean_square()
        scale_rows(4)
        h_tokens()


def shape_constants():
    import numpy as np

    table, dft = np.zeros((P, CONST_N), np.float32), np.zeros((P, DFT_N), np.float32)

    def put(name, a):
        out, (lo, hi) = (table, CONST_AT[name]) if name in CONST_AT else (dft, DFT_AT[name])
        out[:a.shape[0], lo:hi] = a.reshape(a.shape[0], hi - lo)

    i = np.arange(P)
    put("ident", np.eye(P))
    put("pair_sum", np.tile(np.eye(NG), (2, 1)))
    put("ones", np.ones((P, P)))
    col = i % GRID_W
    start = np.clip(col - WIN_COLS // 2, 0, GRID_W - WIN_COLS)[:, None]
    put("mask", np.where((col[None, :] >= start) & (col[None, :] < start + WIN_COLS), 0.0, NEG))
    put("earlier", i[:, None] < i[None, :])
    put("slot_ids", np.tile(np.arange(SLOTS), (P, 1)))
    put("expert_ids", np.tile(np.arange(EXPERTS), (P, 1)))
    u = np.arange(2 * GRID_W - 1)
    z = (np.arange(BIAS_COLS)[:, None] + u[None, :] == WIN_COLS - 1 + GRID_W - 1).astype(np.float32)
    put("diag", z)
    angle = 2 * np.pi * (np.outer(i, i) % P) / P
    put("dft_pos", np.concatenate([np.cos(angle), np.sin(angle)], 1))
    j = np.arange(FGC)
    angle = 2 * np.pi * (np.outer(j, j) % FGC) / FGC
    norm = 1.0 / np.sqrt(P * FGC)
    put("dft_cos", (norm * np.cos(angle)).reshape(2, P, FGC).transpose(1, 0, 2))
    put("dft_sin", (-norm * np.sin(angle)).reshape(2, P, FGC).transpose(1, 0, 2))
    return table, dft


_INS = ["x_prompt", "x_sample", "c", "cache_k", "cache_v", "c_ctx", "ada_w", "ada_b", "norm1_g", "norm2_g", "w_in",
        "conv_w", "rpb", "w_out", "ffn_w1", "ffn_w3", "ffn_w2", "fourier_w", "router_w", "router_b", "moe_w1",
        "moe_w3", "moe_w2", "final_g"]
_OUTS = [((1, P, D), "float32"), ((1, P, D), "float32"), ((1, 1, HEADS, P, HD), "float32"),
         ((1, 1, HEADS, P, HD), "float32")]


def kernel(**inputs):
    import numpy as _np
    import concourse.bacc as _bacc
    from concourse import mybir as _mybir
    from concourse.bass_utils import run_bass_kernel_spmd as _run

    nc = _bacc.Bacc("TRN2", target_bir_lowering=False, num_devices=1)
    arrays, ins, outs = {}, {}, []
    for name in _INS:
        a = _np.ascontiguousarray(inputs[name])
        arrays[f"in_{name}"] = a
        ins[name] = nc.dram_tensor(f"in_{name}", a.shape, _mybir.dt.from_np(a.dtype), kind="ExternalInput").ap()
    tables = []
    for name, table in zip(("shape_constants", "dft_constants"), shape_constants()):
        arrays[name] = table
        tables.append(nc.dram_tensor(name, table.shape, _mybir.dt.float32, kind="ExternalInput").ap())
    for i, (shape, dtype) in enumerate(_OUTS):
        dt = _mybir.dt.from_np(_np.dtype(dtype))
        outs.append(nc.dram_tensor(f"out_{i}", shape, dt, kind="ExternalOutput").ap())
    build(nc, ins, outs, *tables)
    r = _run(nc, [arrays], core_ids=[0])
    return tuple(r.results[0][f"out_{i}"] for i in range(len(_OUTS)))
```

```python
from contextlib import ExitStack

import concourse.bass as bass
from concourse import mybir

F32 = mybir.dt.float32
F32R = mybir.dt.float32r
I32 = mybir.dt.int32
U32 = mybir.dt.uint32
ALU = mybir.AluOpType
ACT = mybir.ActivationFunctionType
AX_X = mybir.AxisListType.X

P = 128
D = 1024
KT = D // P
NG = 2
T = NG * P
HEADS = 8
HD = 64
PAIRS = HEADS // 2
GRID_W = 64
GRID_R = P // GRID_W
WIN_ROWS, WIN_COLS = 8, 16
BIAS_COLS = 2 * WIN_COLS - 1
BIAS_ROWS = 3
CONV_CH = 512
CONV_TAPS = 3
FFN = 2816
EXPERTS = 8
FFE = 3584
EPS = 1e-6
NEG = -1e30
SCALE = HD ** -0.5
FG = 4
FGC = D // FG

COLS = 512
HALF = 2048
RAW = 7
STAGE = 3
AHEAD = STAGE - 1
ROT = 4
FFN_SLICES = -(-FFN // COLS)
MOE_SLICES = FFE // COLS
MOE_HALVES = 6 * MOE_SLICES
SLOTS = 128

CONSTS = [("ident", P), ("ones", P), ("mask", P), ("earlier", P), ("slot_ids", SLOTS), ("expert_ids", EXPERTS),
          ("diag", 2 * GRID_W - 1), ("pair_sum", NG)]
DFT_CONSTS = [("dft_pos", 2 * P), ("dft_cos", 2 * FGC), ("dft_sin", 2 * FGC)]


def placed(table):
    at, out = 0, {}
    for name, n in table:
        out[name] = (at, at + n)
        at += n
    return out, at


CONST_AT, CONST_N = placed(CONSTS)
DFT_AT, DFT_N = placed(DFT_CONSTS)


FFN_ADA = {0: ((0, 11),), 1: ((1, 0),), 2: ((1, 1),), 3: ((1, 2), (1, 3))}


ATT_WHOLE = (4, 5, 6, 7, 8, 9)


def dense_plan():
    plan, whole = [], set()

    def by_rows(name, u):
        for half in range(2):
            plan.append((name, slice(half * D // 2, (half + 1) * D // 2), slice(u * COLS, (u + 1) * COLS)))

    def by_cols(name, c, n=COLS // 2):
        plan.append((name, slice(0, D), slice(c, c + n)))

    def ada(l, units, direct=False):
        for u in units:
            by_rows(f"ada{l}", u)
            if direct:
                whole.update((len(plan) - 2, len(plan) - 1))

    def project(name, u):
        for half in range(2):
            by_cols(name, u * COLS + half * COLS // 2)

    def down(s):
        for r in range(s * COLS, min((s + 1) * COLS, FFN), COLS // 2):
            plan.append(("w2", slice(r, r + COLS // 2), slice(0, D)))

    ada(0, (0, 1), direct=True)
    ada(0, (2, 3))
    project("win", 3)
    project("win", 4)
    by_rows("win", 5)
    for n, u in enumerate((1, 2, 0)):
        for half in range(2):
            by_cols("win", u * COLS + half * COLS // 2)
            ada(0, (4 + 2 * n + half,), direct=4 + 2 * n + half in ATT_WHOLE)
    for u in range(2):
        project("wout", u)
    ada(0, (10,), direct=True)
    for s in range(FFN_SLICES):
        for b, c in enumerate(range(s * COLS, min((s + 1) * COLS, FFN), COLS // 2)):
            by_cols("w1", c)
            by_cols("w3", c)
            for l, u in FFN_ADA.get(2 * s + b, ()):
                ada(l, (u,))
        if s:
            down(s - 1)
    down(FFN_SLICES - 1)
    ada(1, (4, 5), direct=True)
    ada(1, (6, 7, 8))
    project("wf", 0)
    ada(1, (9,))
    project("wf", 1)
    ada(1, (10,), direct=True)
    ada(1, (11,))
    return plan, whole


def moe_plan():
    plan = []
    for s in range(MOE_SLICES):
        plan += [("w1", s, 0), ("w1", s, 1), ("w3", s, 0), ("w3", s, 1)]
        if s:
            plan += [("w2", s - 1, 0), ("w2", s - 1, 1)]
    return plan + [("w2", MOE_SLICES - 1, 0), ("w2", MOE_SLICES - 1, 1)]


PLAN, WHOLE = dense_plan()
MOE_PLAN = moe_plan()
N_PRE = len(PLAN)
SPLIT = [n for n in range(N_PRE) if n not in WHOLE]
N_SPLIT = len(SPLIT)
assert MOE_HALVES % RAW == 0 and MOE_HALVES % STAGE == 0 and len(MOE_PLAN) == MOE_HALVES


def build(nc, ins, outs, consts, dft_consts):
    with ExitStack() as ctx:
        _build(ctx, nc, ins, outs, consts, dft_consts)


def _build(ctx, nc, ins, outs, consts, dft_consts):
    def sb(name, shape, dt=F32):
        return ctx.enter_context(nc.sbuf_tensor(name, shape, dt))

    def sem(name):
        return ctx.enter_context(nc.semaphore(name))

    raw = sb("raw", [P, RAW, HALF])
    w_hi = sb("w_hi", [P, STAGE, HALF], F32R)
    w_lo = sb("w_lo", [P, STAGE, HALF], F32R)
    xT = sb("xT", [P, KT, T])
    hT = sb("hT", [P, KT, T])
    tok = sb("tok", [P, NG, D])
    cst = sb("cst", [P, CONST_N])
    vec_rows = sb("vec_rows", [P, 2, P])
    vecA = sb("vecA", [P, P])
    vecB = sb("vecB", [P, 36])
    cond = sb("cond", [P, KT, NG])
    cond_r = sb("cond_r", [P, 4 * KT + P], F32R)
    mods = sb("mods", [P, 2, 48, NG])
    coef = sb("coef", [P, 4, KT, NG])
    var = sb("var", [P, T])
    rstd = sb("rstd", [P, T])
    router = sb("router", [P, KT, EXPERTS])
    router_bias = sb("router_bias", [P, EXPERTS])
    rpb_rows = sb("rpb_rows", [HEADS * BIAS_ROWS, BIAS_COLS])
    rpbT = sb("rpbT", [BIAS_COLS, HEADS * BIAS_ROWS])
    small = sb("small", [P, 176])
    idx = sb("idx", [P, NG, 8], U32)
    most = sb("most", [P, 1], I32)
    arena = sb("arena", [P, 9728])
    rnd = sb("rnd", [P, 4 * KT * T], F32R)

    free = [0]

    def region(*shape, of=arena):
        n = 1
        for s in shape:
            n *= s
        a = of[:, free[0]:free[0] + n]
        free[0] += n
        assert free[0] <= of.shape[1]
        names = "abcd"[:len(shape)]
        if len(shape) > 1:
            a = a.rearrange(f"p ({' '.join(names)}) -> p {' '.join(names)}", **dict(zip(names, shape)))
        return a

    qT, kT = region(4, T), region(4, T)
    v_tok = region(NG, COLS)
    k_tok = region(COLS)
    conv_u, conv_c = region(4, T), region(4, T)
    kc_tok, vc_tok = region(COLS), region(COLS)
    kcT = region(PAIRS, P)
    bias = region(HEADS, P)
    probs, probsT = region(2, 3 * P), region(2, 3 * P)
    free[0] = 2 * 4 * T + NG * COLS + COLS
    ffn_silu, ffn_prod = region(2, T), region(2, T)
    ffn_end = free[0]
    free[0] = 0
    dftn = region(2, KT, T)
    free[0] = max(free[0], ffn_end)
    dft = region(DFT_N)
    free[0] = 0
    take = region(NG, SLOTS)
    give = region(NG, SLOTS)
    giveT = region(T)
    acc = region(KT, T)
    moe_silu, moe_g = region(2, COLS), region(2, COLS)
    y_slot = region(D)
    free[0] = 0
    h_r = [region(KT, T, of=rnd) for _ in range(2)]
    mix_r = [region(KT, T, of=rnd) for _ in range(2)]
    free[0] = 2 * KT * T
    ffn_r = [region(2, 4, T, of=rnd) for _ in range(2)]
    f_r = h_r
    free[0] = 0
    hg_r = [region(KT, SLOTS, of=rnd) for _ in range(2)]
    gt_r = [region(2, 4, SLOTS, of=rnd) for _ in range(2)]

    def C(name):
        a, b = CONST_AT[name]
        return cst[:, a:b]

    def DFT(name):
        a, b = DFT_AT[name]
        return dft[:, a:b]

    ident, ones, mask, earlier = C("ident"), C("ones"), C("mask"), C("earlier")
    diag = C("diag")[0:BIAS_COLS]
    dft_pos = DFT("dft_pos")
    dft_cos = DFT("dft_cos").rearrange("p (a b) -> p a b", a=2)
    dft_sin = DFT("dft_sin").rearrange("p (a b) -> p a b", a=2)
    ada_rows = tok[0:4].rearrange("p g (i n) -> p (g i) n", i=2)
    ROWS = 4

    neg_max = small[:, 0:4].rearrange("p (a b) -> p a b", a=2)
    row_max = small[:, 4:8].rearrange("p (a b) -> p a b", a=2)
    row_sum = small[:, 8:12].rearrange("p (a b) -> p a b", a=2)
    row_inv = small[:, 12:16].rearrange("p (a b) -> p a b", a=2)
    logits = small[:, 16:32].rearrange("p (g e) -> p g e", g=NG)
    top = small[:, 32:48].rearrange("p (g e) -> p g e", g=NG)
    idx_f = small[:, 48:64].rearrange("p (g e) -> p g e", g=NG)
    gap, gap_exp, gate_den = small[:, 64:66], small[:, 66:68], small[:, 68:70]
    gate_1, gate_2 = small[:, 70:72], small[:, 72:74]
    hot_1 = small[:, 80:96].rearrange("p (g e) -> p g e", g=NG)
    hot_2 = small[:, 96:112].rearrange("p (g e) -> p g e", g=NG)
    chosen = small[:, 112:128].rearrange("p (g e) -> p g e", g=NG)
    gates = small[:, 128:144].rearrange("p (g e) -> p g e", g=NG)
    rank = small[:, 144:160].rearrange("p (g e) -> p g e", g=NG)
    counts = small[:, 160:168]
    most_f = small[:, 168:169]

    ps = ctx.enter_context(nc.psum_tensor("ps", [P, 8, 512], F32))

    raw_full = [sem(f"raw_full{i}") for i in range(RAW)]
    hi_done, lo_done = sem("hi_done"), sem("lo_done")
    part_used = sem("part_used")
    whole_used = sem("whole_used")
    in_vec, in_const, in_x, in_cache, in_small, in_dft = (
        sem(n) for n in ("in_vec", "in_const", "in_x", "in_cache", "in_small", "in_dft"))
    mm_done = sem("mm_done")
    evac_done = sem("evac_done")
    dve_step = sem("dve_step")
    cond_silu, cond_hi, cond_ready = sem("cond_silu"), sem("cond_hi"), sem("cond_ready")
    sq_done = sem("sq_done")
    std_ready = sem("std_ready")
    h_scaled = sem("h_scaled")
    h_ready = sem("h_ready")
    h_round = [sem("h_round_even"), sem("h_round_odd")]
    h_rest = sem("h_rest")
    sc_full, sc_free, mx_ready, exp_done = sem("sc_full"), sem("sc_free"), sem("mx_ready"), sem("exp_done")
    p_ready, pt_full, pt_copied, pv_done = sem("p_ready"), sem("pt_full"), sem("pt_copied"), sem("pv_done")
    up_done, silu_done, g_done, down_done = sem("up_done"), sem("silu_done"), sem("g_done"), sem("down_done")
    tok_full, tok_copied = sem("tok_full"), sem("tok_copied")
    ffn_added = sem("ffn_added")
    chosen_ready = sem("chosen_ready")
    gap_ready, gap_exp_done = sem("gap_ready"), sem("gap_exp_done")
    x_sum = sem("x_sum")
    acc_zero, acc_again = sem("acc_zero"), sem("acc_again")
    most_ready = sem("most_ready")
    rank_moved = sem("rank_moved")
    take_built = sem("take_built")
    give_built = sem("give_built")
    give_full, give_copied = sem("give_full"), sem("give_copied")
    hg_full, hg_hi, hg_lo = sem("hg_full"), sem("hg_hi"), sem("hg_lo")
    e_used = sem("e_used")
    e_silu, e_g = sem("e_silu"), sem("e_g")
    e_turned, gt_hi, gt_lo = sem("e_turned"), sem("gt_hi"), sem("gt_lo")
    y_out = sem("y_out")
    e_spread = sem("e_spread")
    acc_added = sem("acc_added")
    moe_added = sem("moe_added")
    y_ready = sem("y_ready")
    out_kv, out_y = sem("out_kv"), sem("out_y")
    CREDIT = STAGE

    def half_view(buf, slot, h):
        name, rows, cols = h
        r, n = (rows.stop - rows.start) // P, cols.stop - cols.start
        return buf[:, slot, 0:r * n].rearrange("p (k n) -> p k n", n=n)

    def moe_half(name, s, half):
        if name == "w2":
            return name, slice(s * COLS + half * 256, s * COLS + half * 256 + 256), slice(0, D)
        return name, slice(half * D // 2, (half + 1) * D // 2), slice(s * COLS, (s + 1) * COLS)

    used_up = []
    raw_free = {}
    at_turn = {}
    halves_at = {}
    turn_half = []
    att_half = []
    up_half = []
    norm_turn = []

    signal_of_turn = {}

    def turn_half_of(n):
        return turn_half[signal_of_turn[n]]

    def norm_half(k):
        return turn_half_of(norm_turn[k] - 1)

    def ffn_cols(s):
        return min(COLS, FFN - s * COLS)

    block = ctx.enter_context(nc.Block())

    @block.tensor
    def _(pe):
        turn = [0]
        signals = [0]
        parts = [0]
        loads, half_n, wholes = [0], [0], [0]
        near = [0]
        rows_at = {}

        def done(last):
            signal_of_turn[turn[0] - 1] = signals[0]
            signals[0] += 1
            turn_half.append(half_n[0] - near[0])
            last.then_inc(mm_done, 1)

        def bank():
            n = turn[0]
            if n >= ROT:
                pe.wait_ge(evac_done, n - ROT + 1)
            turn[0] += 1
            return ps[:, n % ROT, :]

        def weights(name):
            n = loads[0]
            loads[0] += 1
            i = half_n[0]
            half_n[0] += 1
            assert PLAN[n][0] == name and SPLIT[i] == n, (n, PLAN[n], name)
            pe.wait_ge(lo_done, i + 1)
            raw_free[n] = (lo_done, i + 1)
            return half_view(w_hi, i % STAGE, PLAN[n]), half_view(w_lo, i % STAGE, PLAN[n])

        def whole_weights(name, freed):
            n = loads[0]
            loads[0] += 1
            assert PLAN[n][0] == name and n in WHOLE, (n, PLAN[n], name)
            pe.wait_ge(raw_full[n % RAW], 16 * (n // RAW + 1))
            raw_free[n] = freed
            return half_view(raw, n % RAW, PLAN[n])

        def used_in_part(last):
            parts[0] += 1
            last.then_inc(part_used, 1)
            used_up.append((part_used, parts[0]))

        def mm(out, lhsT, rhs, first, last, **kw):
            return pe.matmul(out, lhsT, rhs, start=first, stop=last, **kw)

        def mm3(out, a, b, first, last, **kw):
            mm(out, a[0], b[0], first, False, **kw)
            mm(out, a[0], b[1], False, False, **kw)
            return mm(out, a[1], b[0], False, last, **kw)

        def transposes(srcs):
            b = bank()
            for i, s in enumerate(srcs):
                n = s.shape[0]
                last = pe.transpose(b[0:s.shape[1], i * n:(i + 1) * n], s, ident[0:n, 0:n])
            done(last)

        def ada_products(l, u):
            b = bank()
            for part in range(2):
                w = weights(f"ada{l}")
                for k in range(4):
                    c = cond_r[:, 4 * (4 * part + k):4 * (4 * part + k) + P]
                    first, end = part == 0 and k == 0, part == 1 and k == 3
                    mm(b, c, w[0][:, k, :], first, False)
                    last = mm(b, c, w[1][:, k, :], False, end)
                if part == 0:
                    used_in_part(last)
            done(last)
            used_up.append((mm_done, signals[0]))
            rows_at[l, u] = len(rows_at) % ROWS, turn[0], 4

        def ada_whole(l, u):
            b = bank()
            for part in range(2):
                if part == 0:
                    wholes[0] += 1
                w = whole_weights(f"ada{l}", (mm_done, signals[0] + 1) if part else (whole_used, wholes[0]))
                for k in range(4):
                    last = mm(b[0:NG], cond[:, 4 * part + k, :], w[:, k, :], part == 0 and k == 0, part == 1 and k == 3)
                if part == 0:
                    last.then_inc(whole_used, 1)
            done(last)
            rows_at[l, u] = len(rows_at) % ROWS, turn[0], NG

        def ada_turn(l, *units):
            for u in units:
                slot, written, n = rows_at[l, u]
                b = bank()
                pe.wait_ge(evac_done, written)
                for j in range(4):
                    last = mm(b[:, NG * j:NG * j + NG], ada_rows[0:n, slot, j * P:(j + 1) * P], C("pair_sum")[0:n],
                              True, True)
                done(last)

        def project(name, src, chunk_hook=None, chunk_ready=None, half_hook=None):
            for part in range(2):
                w = weights(name)
                for j in range(2):
                    b = bank()
                    for k in range(KT):
                        if chunk_ready and part == 0 and j == 0:
                            chunk_ready(k)
                        sl = slice(j * P, (j + 1) * P)
                        last = mm3(b[:, 0:T], (w[0][:, k, sl], w[1][:, k, sl]), (src[0][:, k, :], src[1][:, k, :]),
                                   k == 0, k == KT - 1)
                    done(last)
                    if j == 1:
                        used_up.append((mm_done, signals[0]))
                    if chunk_hook:
                        chunk_hook()
                if half_hook:
                    half_hook()

        def norm_sum(k):
            b = bank()
            for c in range(KT):
                pe.wait_ge(sq_done, KT * k + c + 1)
                last = mm(b[:, 0:T], ones, hT[:, c, :], c == 0, c == KT - 1)
            done(last)
            norm_turn.append(turn[0])

        tokens_n = [0]

        def h_tokens(ready, before=0):
            tokens_n[0] += 1
            for half in range(2):
                pe.wait_ge(ready, before + 4 * (half + 1))
                for g in range(NG):
                    for i in range(4):
                        last = pe.transpose(ps[:, 4 + 2 * half + g, i * P:(i + 1) * P],
                                            hT[:, 4 * half + i, g * P:(g + 1) * P], ident)
                    last.then_inc(tok_full, 1)

        pe.wait_ge(in_const, 16)
        pe.wait_ge(in_vec, 16 * 7)
        transposes([vec_rows[0:36, 1, :]])
        transposes([vec_rows[:, 0, :]])
        def bias_table(q):
            b = bank()
            pe.wait_ge(evac_done, rpb_turn)
            for i in range(16):
                kc = 16 * q + i
                last = mm(b[0:GRID_W, 24 * i:24 * (i + 1)], diag[:, GRID_W - 1 - kc:2 * GRID_W - 1 - kc], rpbT[:],
                          True, True)
            done(last)

        pe.wait_ge(in_x, 32)
        for g in range(NG):
            for half in range(2):
                transposes([tok[:, g, (4 * half + i) * P:(4 * half + i + 1) * P] for i in range(4)])
        at_turn["x"] = turn[0]
        pe.wait_ge(cond_silu, 1)
        ada_whole(0, 0)
        norm_sum(0)
        ada_whole(0, 1)
        pe.wait_ge(in_cache, 32)
        transposes([kc_tok[:, i * P:(i + 1) * P] for i in range(4)])
        pe.wait_ge(in_small, 16 * (HEADS + 2))
        transposes([rpb_rows[:]])
        rpb_turn = turn[0]
        ada_turn(0, 0)
        pe.wait_ge(cond_ready, 1)
        ada_products(0, 2)
        ada_turn(0, 1)
        ada_products(0, 3)
        ada_turn(0, 2, 3)
        bias_table(0)
        bias_table(1)

        def h_chunk(k):
            pe.wait_ge(h_rest, k + 1)

        halves_at["q"] = half_n[0]
        project("win", h_r, chunk_ready=h_chunk)
        bias_table(2)
        bias_table(3)
        project("win", h_r)
        halves_at["v"] = half_n[0]
        banks = [bank(), bank()]
        for part in range(2):
            w = weights("win")
            for g in range(NG):
                for k in range(4):
                    kt = 4 * part + k
                    sl = slice(g * P, (g + 1) * P)
                    last = mm3(banks[g], (h_r[0][:, kt, sl], h_r[1][:, kt, sl]), (w[0][:, k, :], w[1][:, k, :]),
                               kt == 0, kt == KT - 1)
                if part:
                    done(last)
            if part == 0:
                used_in_part(last)
        used_up.append((mm_done, signals[0]))
        pe.wait_ge(evac_done, turn[0] - 2)
        transposes([kT[:, c, 0:P] for c in range(4)])

        def scores(h):
            if h >= 2:
                pe.wait_ge(sc_free, h - 1)
            b, o, c = ps[:, 4 + h % 2, :], HD * (h % 2), h // 2
            for g in range(NG):
                mm(b[:, g * P:(g + 1) * P], qT[o:o + HD, c, g * P:(g + 1) * P], kT[o:o + HD, c, g * P:(g + 1) * P],
                   True, True)
            mm(b[:, 2 * P:3 * P], qT[o:o + HD, c, P:T], kcT[o:o + HD, c, :], True, True).then_inc(sc_full, 1)

        def turn_probs(h):
            pe.wait_ge(p_ready, h + 1)
            if h >= 2:
                pe.wait_ge(pt_copied, h - 1)
            for i in range(3):
                last = pe.transpose(ps[:, 6 + h % 2, i * P:(i + 1) * P], probs[:, h % 2, i * P:(i + 1) * P], ident)
            last.then_inc(pt_full, 1)

        def values(h, b):
            pe.wait_ge(pt_copied, h + 1)
            o, c = HD * (h % 2), HD * h
            pt = probsT[:, h % 2, :]
            mm(b[o:o + HD, 0:P], v_tok[:, 0, c:c + HD], pt[:, 0:P], True, True)
            mm(b[o:o + HD, P:T], v_tok[:, 1, c:c + HD], pt[:, P:T], True, False)
            last = mm(b[o:o + HD, P:T], vc_tok[:, c:c + HD], pt[:, T:T + P], False, True)
            last.then_inc(pv_done, 1)

        step = [0]

        def attention_step():
            i = step[0]
            step[0] += 1
            att_half.append(half_n[0] - near[0])
            if i < HEADS:
                scores(i)
            if 2 <= i < HEADS + 2:
                turn_probs(i - 2)
            if 3 <= i < HEADS + 3 and (i - 3) % 2:
                b = bank()
                values(i - 4, b)
                values(i - 3, b)

        at_turn["cache"] = turn[0]
        near[0] = 1
        gate_unit = [4]

        def attention_ada():
            u = gate_unit[0]
            gate_unit[0] += 1
            (ada_whole if u in ATT_WHOLE else ada_products)(0, u)
            if u > 4:
                ada_turn(0, u - 1)

        for _u in range(3):
            project("win", h_r, attention_step, half_hook=attention_ada)
        near[0] = 0
        ada_turn(0, 9)
        pe.wait_ge(evac_done, turn[0] - 1)
        at_turn["wout"] = turn[0]
        halves_at["wout"] = half_n[0]
        for _u in range(2):
            project("wout", mix_r)
        norm_sum(1)
        ada_whole(0, 10)
        halves_at["ffn"] = half_n[0]

        ups, downs = [0], [0]
        ada_last = [(0, 10)]

        def up(s):
            for pair, c in enumerate(range(0, ffn_cols(s), COLS // 2)):
                banks_ = [4 + (ups[0] + i) % 4 for i in range(2)]
                for n, name in enumerate(("w1", "w3")):
                    w = weights(name)
                    for i in range(2):
                        if n == 0 and ups[0] + i >= 4:
                            pe.wait_ge(g_done, ups[0] + i - 3)
                        for k in range(KT):
                            if s == 0 and c == 0 and n == 0 and i == 0:
                                pe.wait_ge(h_rest, KT + k + 1)
                            sl = slice(i * P, (i + 1) * P)
                            last = mm3(ps[:, banks_[i], n * T:(n + 1) * T], (w[0][:, k, sl], w[1][:, k, sl]),
                                       (h_r[0][:, k, :], h_r[1][:, k, :]), k == 0, k == KT - 1)
                        if n:
                            last.then_inc(up_done, 1)
                            up_half.append(half_n[0])
                    if n:
                        used_up.append((up_done, ups[0] + 2))
                    else:
                        used_in_part(last)
                ups[0] += 2
                for unit in FFN_ADA.get(2 * s + pair, ()):
                    ada_turn(*ada_last[0])
                    ada_products(*unit)
                    ada_last[0] = unit

        def down(s):
            for part in range(ffn_cols(s) * 2 // COLS):
                w = weights("w2")
                for i in range(2):
                    f = 2 * part + i
                    pe.wait_ge(g_done, 4 * s + f + 1)
                    for o in range(KT):
                        sl = slice(o * P, (o + 1) * P)
                        last = mm3(ps[:, o // 2, (o % 2) * T:(o % 2 + 1) * T], (w[0][:, i, sl], w[1][:, i, sl]),
                                   (ffn_r[0][:, s % 2, f, :], ffn_r[1][:, s % 2, f, :]),
                                   s == 0 and f == 0 and o % 2 == 0, 4 * s + f == FFN // P - 1, skip_group_check=True)
                last.then_inc(down_done, 1)
                downs[0] += 1
                used_up.append((down_done, downs[0]))

        up(0)
        up(1)
        ada_turn(*ada_last[0])
        pe.wait_ge(evac_done, turn[0])
        down(0)
        for s in range(2, FFN_SLICES):
            up(s)
            down(s - 1)
        down(FFN_SLICES - 1)
        halves_at["ffn_end"] = half_n[0]

        pe.wait_ge(ffn_added, 2 * (turn[0] % ROT + 1))
        ada_whole(1, 4)
        pe.wait_ge(ffn_added, KT)
        norm_sum(2)
        ada_whole(1, 5)
        ada_turn(1, 4, 5)
        halves_at["fourier"] = half_n[0]
        h_tokens(h_ready, 2 * KT)
        pe.wait_ge(in_dft, 16)
        pe.wait_ge(tok_copied, 4 * tokens_n[0])
        for g in range(NG):
            for cp in range(4):
                b = bank()
                for i in range(2):
                    c = 2 * cp + i
                    last = mm(b[:, i * T:(i + 1) * T], tok[:, g, c * P:(c + 1) * P], dft_pos, True, True)
                done(last)
        dftn_written = turn[0]
        ada_products(1, 6)
        pe.wait_ge(evac_done, dftn_written)
        for o in range(KT):
            grp, oc = o // 2, o % 2
            b = bank()
            for n, mat in enumerate((dft_cos, dft_sin)):
                for ic in range(2):
                    last = mm(b[:, 0:T], mat[:, ic, oc * P:(oc + 1) * P], dftn[:, n, 2 * grp + ic, :],
                              n == 0 and ic == 0, n == 1 and ic == 1)
            done(last)
        f_written = turn[0]
        ada_products(1, 7)
        ada_turn(1, 6)
        ada_products(1, 8)
        ada_turn(1, 7)
        pe.wait_ge(evac_done, f_written)
        at_turn["wf"] = turn[0]
        project("wf", f_r)
        ada_products(1, 9)
        ada_turn(1, 8)
        at_turn["wf_1"] = turn[0]
        project("wf", f_r)
        ada_turn(1, 9)
        norm_sum(3)
        ada_whole(1, 10)
        ada_products(1, 11)
        ada_turn(1, 10, 11)
        halves_at["router"] = half_n[0]

        at_turn["router"] = turn[0]
        pe.wait_ge(h_ready, 4 * KT)
        b = bank()
        for g in range(NG):
            for k in range(KT):
                last = mm(b[:, EXPERTS * g:EXPERTS * (g + 1)], hT[:, k, g * P:(g + 1) * P], router[:, k, :],
                          k == 0, k == KT - 1)
                if g == 0 and k == 0:
                    last.then_inc(e_used, CREDIT)
        done(last)
        h_tokens(h_ready, 3 * KT)
        pe.wait_ge(chosen_ready, 1)
        b = bank()
        mm(b[:, 0:8], earlier, chosen[:, 0, :], True, True)
        mm(b[:, 8:16], earlier, chosen[:, 1, :], True, False)
        mm(b[:, 8:16], ones, chosen[:, 0, :], False, True)
        mm(b[:, 16:24], ones, chosen[:, 0, :], True, False)
        done(mm(b[:, 16:24], ones, chosen[:, 1, :], False, True))
        pe.wait_ge(evac_done, turn[0])
        pe.wait_ge(tok_copied, 4 * tokens_n[0])

        def gather(job, banks_ready=None):
            pe.wait_ge(take_built, job + 1)
            for q in range(2):
                b = ps[:, 6 + q, :]
                if q == 1 and banks_ready:
                    banks_ready()
                for i in range(4):
                    c = 4 * q + i
                    for g in range(NG):
                        last = mm(b[:, i * SLOTS:(i + 1) * SLOTS], tok[:, g, c * P:(c + 1) * P],
                                  take[:, g, :], g == 0, g == NG - 1)
                last.then_inc(hg_full, 1)

        def expert(job, last_one=False):
            at = [0]

            def half():
                i = at[0]
                at[0] += 1
                slot = (N_SPLIT + i) % STAGE
                pe.wait_ge(lo_done, N_SPLIT + i + 1 + MOE_HALVES * job)
                h = moe_half(*MOE_PLAN[i])
                return half_view(w_hi, slot, h), half_view(w_lo, slot, h)

            def up(s, n):
                b = ps[:, 2 + 2 * (s % 2) + n, :]
                for part in range(2):
                    w = half()
                    for k in range(4):
                        kt = 4 * part + k
                        last = mm3(b, (hg_r[0][:, kt, :], hg_r[1][:, kt, :]), (w[0][:, k, :], w[1][:, k, :]),
                                   kt == 0, kt == KT - 1)
                    last.then_inc(e_used, 1)

            def turn_g(s):
                pe.wait_ge(e_g, MOE_SLICES * job + s + 1)
                b = ps[:, 6 + s % 2, :]
                for i in range(4):
                    last = pe.transpose(b[:, i * SLOTS:(i + 1) * SLOTS], moe_g[:, s % 2, i * P:(i + 1) * P], ident)
                last.then_inc(e_turned, 1)

            def down(s, part):
                w = half()
                pe.wait_ge(gt_lo, MOE_SLICES * job + s + 1)
                for i in range(2):
                    f = 2 * part + i
                    for o in range(2):
                        sl = slice(o * COLS, (o + 1) * COLS)
                        last = mm3(ps[:, o, :], (gt_r[0][:, s % 2, f, :], gt_r[1][:, s % 2, f, :]),
                                   (w[0][:, i, sl], w[1][:, i, sl]), s == 0 and f == 0,
                                   s == MOE_SLICES - 1 and f == 3)
                last.then_inc(e_used, 1)

            pe.wait_ge(hg_lo, 2 * (job + 1))
            for s in range(MOE_SLICES):
                if s == 0:
                    pe.wait_ge(acc_added, 4 * job - 2 + CREDIT)
                elif s == 1:
                    pe.wait_ge(acc_added, 4 * job + CREDIT)
                else:
                    pe.wait_ge(e_g, MOE_SLICES * job + s - 1)
                up(s, 0)
                if s:
                    turn_g(s - 1)
                up(s, 1)
                if 0 < s < MOE_SLICES - 1:
                    down(s - 1, 0)
                    down(s - 1, 1)
            if not last_one:
                gather(job + 1, lambda: pe.wait_ge(gt_lo, MOE_SLICES * job + MOE_SLICES - 1))
            down(MOE_SLICES - 2, 0)
            if not last_one:
                pe.wait_ge(hg_lo, 2 * (job + 1) + 1)
            turn_g(MOE_SLICES - 1)
            down(MOE_SLICES - 2, 1)
            down(MOE_SLICES - 1, 0)
            pe.wait_ge(give_built, job + 1)
            if not last_one:
                pe.wait_ge(hg_lo, 2 * (job + 1) + 2)
            for g in range(NG):
                last = pe.transpose(ps[0:SLOTS, 7, g * P:(g + 1) * P], give[:, g, :], ident)
            last.then_inc(give_full, 1)
            down(MOE_SLICES - 1, 1)
            pe.wait_ge(give_copied, job + 1)
            for q in range(4):
                if q % 2 == 0:
                    pe.wait_ge(y_out, 2 * job + q // 2 + 1)
                for i in range(2):
                    c = 2 * q + i
                    last = mm(ps[:, 2 + q, i * T:(i + 1) * T], y_slot[:, c * P:(c + 1) * P], giveT, True, True)
                last.then_inc(e_spread, 1)

        gather(0)
        with pe.Fori(0, EXPERTS - 1) as e:
            expert(e)
        expert(EXPERTS - 1, last_one=True)
        most_here = pe.value_load(most[0:1, 0:1], min_val=0, max_val=T)
        with pe.If(most_here > SLOTS):
            pe.wait_ge(moe_added, KT)
            gather(EXPERTS)
            with pe.Fori(EXPERTS, 2 * EXPERTS - 1) as job:
                expert(job)
            expert(2 * EXPERTS - 1, last_one=True)
        norm_sum(4)
        h_tokens(y_ready)

    @block.sync
    def _(sp):
        dense = {"ada0": ins["ada_w"][0], "ada1": ins["ada_w"][1], "win": ins["w_in"][0], "wout": ins["w_out"][0],
                 "wf": ins["fourier_w"][0], "w1": ins["ffn_w1"][0], "w3": ins["ffn_w3"][0], "w2": ins["ffn_w2"][0]}
        vec_loads = [(0, 1, KT, ins["c_ctx"].rearrange("(k p) -> k p", p=P)),
                     (8, 1, KT, ins["c"][0].rearrange("(k p) -> k p", p=P)),
                     (16, 1, KT, ins["final_g"].rearrange("(k p) -> k p", p=P)),
                     (24, 1, 12, ins["conv_w"][0].rearrange("j (k p) -> (j k) p", p=P)),
                     (0, 0, 96, ins["ada_b"].rearrange("l (k p) -> (l k) p", p=P)),
                     (96, 0, 16, ins["norm1_g"].rearrange("l (k p) -> (l k) p", p=P)),
                     (112, 0, 16, ins["norm2_g"].rearrange("l (k p) -> (l k) p", p=P))]
        for at, tile, n, src in vec_loads:
            sp.dma_start(vec_rows[at:at + n, tile, :], src).then_inc(in_vec, 16)
        sp.dma_start(cst[:], consts).then_inc(in_const, 16)
        sp.dma_start(tok[:, 0, :], ins["x_prompt"][0]).then_inc(in_x, 16)
        sp.dma_start(tok[:, 1, :], ins["x_sample"][0]).then_inc(in_x, 16)
        for n, (name, rows, cols) in enumerate(PLAN):
            if n >= RAW:
                sp.wait_ge(*raw_free[n - RAW])
            sp.dma_start(half_view(raw, n % RAW, PLAN[n]),
                         dense[name][rows, cols].rearrange("(k p) n -> p k n", p=P)).then_inc(raw_full[n % RAW], 16)

        def load_expert(job, e):
            for i, h in enumerate(MOE_PLAN):
                name, rows, cols = moe_half(*h)
                slot = (N_PRE + i) % RAW
                if i < RAW:
                    sp.wait_ge(*raw_free[N_PRE + i - RAW])
                sp.wait_ge(lo_done, N_SPLIT + i - RAW + 1 + MOE_HALVES * job)
                src = ins["moe_" + name][0, bass.ds(e, 1), rows, cols].rearrange("o (k p) n -> p (o k) n", p=P)
                sp.dma_start(half_view(raw, slot, (name, rows, cols)), src).then_inc(raw_full[slot], 16)

        with sp.Fori(0, EXPERTS) as e:
            load_expert(e, e)
        sp.wait_ge(most_ready, 1)
        most_here = sp.value_load(most[0:1, 0:1], min_val=0, max_val=T)
        with sp.If(most_here > SLOTS):
            with sp.Fori(0, EXPERTS) as e:
                load_expert(e + EXPERTS, e)
        for half in range(2):
            for g in range(NG):
                sp.wait_ge(tok_copied, 8 + 2 * half + g + 1)
                sl = slice(half * COLS, (half + 1) * COLS)
                sp.dma_start(outs[g][0][:, sl], tok[:, g, sl]).then_inc(out_y, 16)
        sp.wait_ge(out_y, 64)

    @block.gpsimd
    def _(pool):
        def round_h(k):
            for c in range(0, KT, 2):
                pool.wait_ge(h_ready, KT * k + c + 1)
                pool.tensor_copy(h_r[0][:, c, :], hT[:, c, :]).then_inc(h_round[0], 1)

        pool.dma_start(kc_tok.rearrange("l (h d) -> l h d", h=HEADS),
                      ins["cache_k"][0, 0].rearrange("h l d -> l h d")).then_inc(in_cache, 16)
        pool.dma_start(vc_tok.rearrange("l (h d) -> l h d", h=HEADS),
                      ins["cache_v"][0, 0].rearrange("h l d -> l h d")).then_inc(in_cache, 16)
        for h in range(HEADS):
            pool.dma_start(rpb_rows[BIAS_ROWS * h:BIAS_ROWS * (h + 1), :],
                          ins["rpb"][0, h, WIN_ROWS - 2:WIN_ROWS + 1, :]).then_inc(in_small, 16)
        pool.dma_start(router[:], ins["router_w"][0].rearrange("(k p) e -> p k e", p=P)).then_inc(in_small, 16)
        pool.dma_start(router_bias[:], ins["router_b"][0:1, :].to_broadcast([P, EXPERTS])).then_inc(in_small, 16)
        round_h(0)
        pool.wait_ge(evac_done, at_turn["cache"])
        for n, src in ((2, k_tok), (3, v_tok[:, 0, :])):
            pool.dma_start(outs[n][0, 0].rearrange("h s d -> s h d"),
                           src.rearrange("s (h d) -> s h d", h=HEADS)).then_inc(out_kv, 16)
        pool.wait_ge(out_kv, 32)
        pool.wait_ge(evac_done, at_turn["wout"])
        pool.dma_start(dft, dft_consts).then_inc(in_dft, 16)
        pool.wait_ge(in_dft, 16)
        round_h(1)
        pool.wait_ge(evac_done, at_turn["router"])
        pool.memset(acc, 0.0).then_inc(acc_zero, 1)

    @block.scalar
    def _(act):
        split = [0]

        def split_ahead(used):
            while split[0] < min(used + AHEAD, N_SPLIT):
                i = split[0]
                split[0] += 1
                n = SPLIT[i]
                act.wait_ge(raw_full[n % RAW], 16 * (n // RAW + 1))
                if i >= STAGE:
                    act.wait_ge(*used_up[i - STAGE])
                act.activation(half_view(w_hi, i % STAGE, PLAN[n]), half_view(raw, n % RAW, PLAN[n]),
                               ACT.Copy).then_inc(hi_done, 1)

        act.wait_ge(evac_done, 1)
        act.activation(cond[:].rearrange("p k v -> p v k"), vecB[:, 0:16].rearrange("p (v k) -> p v k", v=NG),
                       ACT.Silu).then_inc(cond_silu, 1)
        act.wait_ge(cond_silu, 1)
        act.wait_ge(cond_hi, 1)
        act.activation(cond_r[:, 0:4 * KT].rearrange("p (k v) -> p k v", v=4)[:, :, 0:2], cond[:],
                       ACT.Copy).then_inc(cond_silu, 1)

        def norm(k, ready, first, used):
            for c in range(KT):
                act.wait_ge(ready, first(c))
                act.activation(hT[:, c, :], xT[:, c, :], ACT.Square).then_inc(sq_done, 1)
            split_ahead(used)
            act.wait_ge(evac_done, norm_turn[k])
            act.activation(var[:], var[:], ACT.Sqrt).then_inc(std_ready, 1)
            if k == 0:
                split_ahead(halves_at["q"])
            if k < 4:
                l, half = k // 2, k % 2
                for c in range(KT):
                    act.wait_ge(h_scaled, KT * k + c + 1)
                    for g in range(NG):
                        sl = slice(g * P, (g + 1) * P)
                        last = act.activation(hT[:, c, sl], hT[:, c, sl], ACT.Identity, scale=coef[:, k, c, g:g + 1],
                                              bias=mods[:, l, 24 * half + c, g:g + 1])
                    last.then_inc(h_ready, 1)
                    if k < 2 and c % 2:
                        act.wait_ge(h_ready, KT * k + c + 1)
                        act.activation(h_r[0][:, c, :], hT[:, c, :], ACT.Copy).then_inc(h_round[1], 1)

        tokens_n = [0]

        def h_tokens():
            for q in range(4):
                act.wait_ge(tok_full, tokens_n[0] + 1)
                tokens_n[0] += 1
                act.activation(tok[:, q % 2, (q // 2) * COLS:(q // 2 + 1) * COLS], ps[:, 4 + q, :],
                               ACT.Copy).then_inc(tok_copied, 1)

        norm(0, evac_done, lambda c: at_turn["x"], 0)
        for i in range(12):
            split_ahead(att_half[i])
            if i < HEADS:
                act.wait_ge(mx_ready, i + 1)
                act.activation(probs[:, i % 2, 0:P], probs[:, i % 2, 0:P], ACT.Exp, bias=neg_max[:, i % 2, 0:1],
                               accum_out=row_sum[:, i % 2, 0:1])
                act.activation(probs[:, i % 2, P:3 * P], probs[:, i % 2, P:3 * P], ACT.Exp,
                               bias=neg_max[:, i % 2, 1:2], accum_out=row_sum[:, i % 2, 1:2]).then_inc(exp_done, 1)
            if 2 <= i < HEADS + 2:
                h = i - 2
                act.wait_ge(pt_full, h + 1)
                if h >= 2:
                    act.wait_ge(pv_done, h - 1)
                act.activation(probsT[:, h % 2, :], ps[:, 6 + h % 2, 0:3 * P], ACT.Copy).then_inc(pt_copied, 1)
        split_ahead(halves_at["wout"])

        def wout_chunk(c):
            split_ahead(turn_half_of(at_turn["wout"] + c))
            return at_turn["wout"] + c + 1

        def wf_chunk(c):
            t = at_turn["wf"] + c if c < 4 else at_turn["wf_1"] + c - 4
            split_ahead(turn_half_of(t))
            return t + 1

        def ffn_chunk(c):
            split_ahead(halves_at["ffn_end"])
            return c + 1

        norm(1, evac_done, wout_chunk, norm_half(1))
        act.wait_ge(out_kv, 32)
        for a in range(FFN // P):
            split_ahead(up_half[a])
            act.wait_ge(up_done, a + 1)
            if a >= 2:
                act.wait_ge(g_done, a - 1)
            act.activation(ffn_silu[:, a % 2, :], ps[:, 4 + a % 4, 0:T], ACT.Silu).then_inc(silu_done, 1)
        norm(2, ffn_added, ffn_chunk, norm_half(2))
        h_tokens()
        norm(3, evac_done, wf_chunk, norm_half(3))
        split_ahead(N_SPLIT)
        def hg_round(job, q):
            act.wait_ge(hg_full, 2 * job + q + 1)
            act.activation(hg_r[0][:, 4 * q:4 * q + 4, :], ps[:, 6 + q, :].rearrange("p (c s) -> p c s", c=4),
                           ACT.Copy).then_inc(hg_hi, 1)

        def split_half(job, i):
            slot, m = (N_SPLIT + i) % STAGE, N_PRE + i
            act.wait_ge(raw_full[m % RAW], 16 * (m // RAW + 1) + 16 * (MOE_HALVES // RAW) * job)
            act.wait_ge(e_used, MOE_HALVES * job + i - STAGE + 1 + CREDIT)
            act.activation(w_hi[:, slot, :], raw[:, m % RAW, :], ACT.Copy).then_inc(hi_done, 1)

        def expert(job, last_one=False):
            at = [STAGE]

            def split_to(n):
                while at[0] < n:
                    split_half(job, at[0])
                    at[0] += 1

            def silu(s):
                act.wait_ge(e_used, MOE_HALVES * job + MOE_PLAN.index(("w1", s, 1)) + 1 + CREDIT)
                act.activation(moe_silu[:, s % 2, :], ps[:, 2 + 2 * (s % 2), :], ACT.Silu).then_inc(e_silu, 1)

            def gt_round(s):
                act.wait_ge(e_turned, MOE_SLICES * job + s + 1)
                act.activation(gt_r[0][:, s % 2, :, :], ps[:, 6 + s % 2, :].rearrange("p (f s) -> p f s", f=4),
                               ACT.Copy).then_inc(gt_hi, 1)

            split_to(4)
            silu(0)
            split_to(6)
            for s in range(1, MOE_SLICES):
                base = MOE_PLAN.index(("w1", s, 0))
                split_to(base + 4)
                silu(s)
                gt_round(s - 1)
                split_to(base + 6)
            if not last_one:
                hg_round(job + 1, 0)
                hg_round(job + 1, 1)
            split_to(MOE_HALVES - 1)
            gt_round(MOE_SLICES - 1)
            split_to(MOE_HALVES)
            if not last_one:
                split_half(job + 1, 0)
            act.wait_ge(give_full, job + 1)
            act.activation(giveT, ps[:, 7, 0:T], ACT.Copy).then_inc(give_copied, 1)
            if not last_one:
                split_half(job + 1, 1)
            act.wait_ge(e_used, MOE_HALVES * job + MOE_HALVES + CREDIT)
            for o in range(2):
                act.activation(y_slot[:, o * COLS:(o + 1) * COLS], ps[:, o, :], ACT.Copy).then_inc(y_out, 1)
            if not last_one:
                split_half(job + 1, 2)

        split_half(0, 0)
        h_tokens()
        act.wait_ge(gap_ready, 1)
        act.activation(gap_exp, gap, ACT.Exp).then_inc(gap_exp_done, 1)
        for i in range(1, STAGE):
            split_half(0, i)
        for q in range(2):
            hg_round(0, q)
        with act.Fori(0, EXPERTS - 1) as e:
            expert(e)
        expert(EXPERTS - 1, last_one=True)
        most_here = act.value_load(most[0:1, 0:1], min_val=0, max_val=T)
        with act.If(most_here > SLOTS):
            for i in range(STAGE):
                split_half(EXPERTS, i)
            for q in range(2):
                hg_round(EXPERTS, q)
            with act.Fori(EXPERTS, 2 * EXPERTS - 1) as job:
                expert(job)
            expert(2 * EXPERTS - 1, last_one=True)
            act.wait_ge(moe_added, 2 * KT)
        norm(4, moe_added, lambda c: c + 1, N_SPLIT)
        h_tokens()

    @block.vector
    def _(dve):
        turn = [0]
        signals = [0]
        steps = [0]
        split = [0]

        def split_ahead(used):
            while split[0] < min(used + AHEAD, N_SPLIT):
                i = split[0]
                split[0] += 1
                n = SPLIT[i]
                dve.wait_ge(hi_done, i + 1)
                dve.tensor_tensor(half_view(w_lo, i % STAGE, PLAN[n]), half_view(raw, n % RAW, PLAN[n]),
                                  half_view(w_hi, i % STAGE, PLAN[n]).bitcast(F32), ALU.subtract).then_inc(lo_done, 1)

        def full(heads=None, near=0):
            n = turn[0]
            turn[0] += 1
            if heads is None:
                if turn_half[signals[0]]:
                    split_ahead(turn_half[signals[0]] - near)
                signals[0] += 1
                dve.wait_ge(mm_done, signals[0])
            else:
                dve.wait_ge(pv_done, heads)
            return ps[:, n % ROT, :]

        def link(ins_):
            steps[0] += 1
            ins_.then_inc(dve_step, 1)
            dve.wait_ge(dve_step, steps[0])

        def copy_turn(dst, view):
            b = full()
            dve.tensor_copy(dst, view(b)).then_inc(evac_done, 1)

        def split_turn(dst, b):
            link(dve.tensor_copy(dst[0], b))
            dve.tensor_tensor(dst[1], b, dst[0].bitcast(F32), ALU.subtract).then_inc(evac_done, 1)

        def mod(l, part):
            return mods[:, l, 8 * part:8 * part + 8, :]

        rows_n = [0]

        def ada_rows_out(whole=False):
            slot = rows_n[0] % ROWS
            rows_n[0] += 1
            n = NG if whole else 4
            dve.tensor_copy(ada_rows[0:n, slot, :], full(near=1)[0:n, :]).then_inc(evac_done, 1)

        def ada_mods(l, *units):
            for u in units:
                b = full()
                bias_ = vecA[:, 48 * l + 4 * u:48 * l + 4 * u + 4]
                bias_ = bias_.rearrange("p (c o) -> p c o", o=1).to_broadcast([P, 4, NG])
                dve.tensor_tensor(mods[:, l, 4 * u:4 * u + 4, :], b[:, 0:8].rearrange("p (c v) -> p c v", c=4),
                                  bias_, ALU.add).then_inc(evac_done, 1)

        def coefs(k):
            l, half = k // 2, k % 2
            g = vecA[:, 96 + 16 * half + 8 * l:96 + 16 * half + 8 * l + 8]
            dve.wait_ge(evac_done, turn[0])
            link(dve.scalar_tensor_tensor(coef[:, k, :, :], mod(l, 3 * half + 1), 1.0,
                                          g.rearrange("p (c o) -> p c o", o=1).to_broadcast([P, KT, NG]),
                                          ALU.add, ALU.mult))

        def mean_square():
            b = full()
            dve.tensor_scalar(var[:], b[:, 0:T], 1.0 / D, EPS, ALU.mult, ALU.add).then_inc(evac_done, 1)

        def scale_rows(k):
            dve.wait_ge(std_ready, k + 1)
            link(dve.reciprocal(rstd[:], var[:]))
            lag = 3
            for c in range(KT + lag):
                if c < KT and k < 4:
                    dve.tensor_tensor(hT[:, c, :], xT[:, c, :], rstd[:], ALU.mult).then_inc(h_scaled, 1)
                elif c < KT:
                    dve.scalar_tensor_tensor(hT[:, c, :], xT[:, c, :], vecB[:, 16 + c:17 + c], rstd[:], ALU.mult,
                                             ALU.mult).then_inc(y_ready, 1)
                if k < 2 and c >= lag:
                    d = c - lag
                    dve.wait_ge(h_round[d % 2], KT // 2 * k + d // 2 + 1)
                    dve.tensor_tensor(h_r[1][:, d, :], hT[:, d, :], h_r[0][:, d, :].bitcast(F32),
                                      ALU.subtract).then_inc(h_rest, 1)

        def residual(l, part, chunks):
            for c in chunks:
                b = full()
                for g in range(NG):
                    sl = slice(g * P, (g + 1) * P)
                    last = dve.scalar_tensor_tensor(xT[:, c, sl], b[:, sl], mods[:, l, 8 * part + c, g:g + 1],
                                                    xT[:, c, sl], ALU.mult, ALU.add)
                last.then_inc(evac_done, 1)

        dve.memset(cond_r[:].bitcast(F32), 0.0).then_inc(cond_hi, 1)
        copy_turn(vecB[:], lambda b: b[:, 0:36])
        copy_turn(vecA[:], lambda b: b[:, 0:P])

        def bias_table(q):
            b = full()[:, 0:384].rearrange("p (k h r) -> p h k r", h=HEADS, r=BIAS_ROWS)
            for qr in range(GRID_R):
                rows = slice(qr * GRID_W, (qr + 1) * GRID_W)
                for kr in range(GRID_R):
                    cols = slice(kr * GRID_W + 16 * q, kr * GRID_W + 16 * q + 16)
                    m = mask[0:GRID_W, cols].rearrange("p (o k) -> p o k", o=1).to_broadcast([GRID_W, HEADS, 16])
                    last = dve.tensor_tensor(bias[rows, :, cols], b[0:GRID_W, :, :, kr - qr + 1], m, ALU.add)
            last.then_inc(evac_done, 1)

        for g in range(NG):
            for half in range(2):
                copy_turn(xT[:, 4 * half:4 * half + 4, g * P:(g + 1) * P],
                          lambda b: b.rearrange("p (c t) -> p c t", c=4))
        dve.wait_ge(cond_silu, 2)
        cond_v = cond_r[:, 0:4 * KT].rearrange("p (k v) -> p k v", v=4)
        dve.tensor_tensor(cond_v[:, :, 2:4], cond[:], cond_v[:, :, 0:2].bitcast(F32), ALU.subtract).then_inc(cond_ready, 1)
        ada_rows_out(whole=True)
        mean_square()
        split_ahead(0)
        ada_rows_out(whole=True)
        copy_turn(kcT, lambda b: b.rearrange("p (c t) -> p c t", c=4))
        copy_turn(rpbT[:], lambda b: b[0:BIAS_COLS, 0:24])
        ada_mods(0, 0)
        ada_rows_out()
        ada_mods(0, 1)
        ada_rows_out()
        ada_mods(0, 2, 3)
        coefs(0)
        scale_rows(0)
        bias_table(0)
        bias_table(1)
        for c in range(4):
            copy_turn(qT[:, c, :], lambda b: b[:, 0:T])
        bias_table(2)
        bias_table(3)
        for c in range(4):
            copy_turn(kT[:, c, :], lambda b: b[:, 0:T])
        for g in range(NG):
            copy_turn(v_tok[:, g, :], lambda b: b)
        copy_turn(k_tok, lambda b: b)

        def soften(h):
            dve.wait_ge(sc_full, h + 1)
            if h >= 2:
                dve.wait_ge(pt_full, h - 1)
            b = ps[:, 4 + h % 2, 0:3 * P].rearrange("p (n t) -> p n t", n=3)
            s = probs[:, h % 2, :].rearrange("p (n t) -> p n t", n=3)
            dve.tensor_scalar(s[:, 0:3:2, :], b[:, 0:3:2, :], SCALE, None, ALU.mult)
            dve.scalar_tensor_tensor(s[:, 1, :], b[:, 1, :], SCALE, bias[:, h, :], ALU.mult, ALU.add).then_inc(sc_free, 1)
            dve.wait_ge(sc_free, h + 1)
            dve.reduce_max(row_max[:, h % 2, 0:1], probs[:, h % 2, 0:P], AX_X)
            link(dve.reduce_max(row_max[:, h % 2, 1:2], probs[:, h % 2, P:3 * P], AX_X))
            dve.tensor_scalar(neg_max[:, h % 2, :], row_max[:, h % 2, :], -1.0, None, ALU.mult).then_inc(mx_ready, 1)

        def normalise(h):
            dve.wait_ge(exp_done, h + 1)
            link(dve.reciprocal(row_inv[:, h % 2, :], row_sum[:, h % 2, :]))
            dve.tensor_scalar(probs[:, h % 2, 0:P], probs[:, h % 2, 0:P], row_inv[:, h % 2, 0:1], None, ALU.mult)
            dve.tensor_scalar(probs[:, h % 2, P:3 * P], probs[:, h % 2, P:3 * P], row_inv[:, h % 2, 1:2], None,
                              ALU.mult).then_inc(p_ready, 1)

        def tap(j, c):
            return vecB[:, 24 + 4 * j + c:25 + 4 * j + c]

        def convolve(c):
            u = conv_u[:, c, :].rearrange("p (g t) -> p g t", g=NG)
            y = conv_c[:, c, :].rearrange("p (g t) -> p g t", g=NG)
            link(dve.tensor_scalar(y, u, tap(1, c), None, ALU.mult))
            link(dve.scalar_tensor_tensor(y[:, :, 1:P], u[:, :, 0:P - 1], tap(0, c), y[:, :, 1:P], ALU.mult, ALU.add))
            link(dve.scalar_tensor_tensor(y[:, :, 0:P - 1], u[:, :, 1:P], tap(2, c), y[:, :, 0:P - 1], ALU.mult, ALU.add))

        for i in range(12):
            b = full()
            part, c = i // 4, i % 4
            if part == 0:
                dve.tensor_copy(conv_c[:, c, :], b[:, 0:T]).then_inc(evac_done, 1)
            elif part == 1:
                dve.tensor_tensor(conv_u[:, c, :], b[:, 0:T], conv_c[:, c, :], ALU.mult).then_inc(evac_done, 1)
            else:
                dve.tensor_tensor(conv_u[:, c, :], b[:, 0:T], conv_c[:, c, :], ALU.mult).then_inc(evac_done, 1)
            if i < HEADS:
                soften(i)
            if 1 <= i < HEADS + 1:
                normalise(i - 1)
            if part == 1:
                dve.wait_ge(evac_done, turn[0])
                convolve(c)
            elif part == 2:
                dve.wait_ge(evac_done, turn[0])
                link(dve.tensor_copy(mix_r[0][:, c, :], conv_u[:, c, :]))
                dve.tensor_tensor(mix_r[1][:, c, :], conv_u[:, c, :], mix_r[0][:, c, :].bitcast(F32), ALU.subtract)
            if 3 <= i < HEADS + 3 and (i - 3) % 2:
                c = 4 + (i - 3) // 2
                split_turn((mix_r[0][:, c, :], mix_r[1][:, c, :]), full(i - 2)[:, 0:T])
            if i % 2:
                ada_rows_out(whole=4 + i // 2 in ATT_WHOLE)
                if i > 1:
                    ada_mods(0, 4 + i // 2 - 1)
        ada_mods(0, 9)
        dve.wait_ge(evac_done, turn[0])
        residual(0, 2, range(KT))
        coefs(1)
        mean_square()
        split_ahead(norm_half(1))
        scale_rows(1)
        ada_rows_out(whole=True)
        ada_last = (0, 10)
        for a in range(FFN // P):
            s, f = a // 4, a % 4
            split_ahead(up_half[a])
            dve.wait_ge(silu_done, a + 1)
            link(dve.tensor_tensor(ffn_prod[:, a % 2, :], ps[:, 4 + a % 4, T:2 * T], ffn_silu[:, a % 2, :], ALU.mult))
            link(dve.tensor_copy(ffn_r[0][:, s % 2, f, :], ffn_prod[:, a % 2, :]))
            dve.tensor_tensor(ffn_r[1][:, s % 2, f, :], ffn_prod[:, a % 2, :], ffn_r[0][:, s % 2, f, :].bitcast(F32),
                              ALU.subtract).then_inc(g_done, 1)
            if a % 2:
                for unit in FFN_ADA.get(a // 2, ()):
                    ada_mods(*ada_last)
                    ada_rows_out()
                    ada_last = unit
                if a // 2 == max(FFN_ADA):
                    ada_mods(*ada_last)
        split_ahead(halves_at["ffn_end"])
        dve.wait_ge(down_done, FFN // (COLS // 2))
        dve.wait_ge(evac_done, turn[0])
        for c in range(KT):
            for g in range(NG):
                sl = slice(g * P, (g + 1) * P)
                off = (c % 2) * T + g * P
                last = dve.scalar_tensor_tensor(xT[:, c, sl], ps[:, c // 2, off:off + P], mods[:, 0, 40 + c, g:g + 1],
                                                xT[:, c, sl], ALU.mult, ALU.add)
            last.then_inc(ffn_added, 1)
        coefs(2)
        ada_rows_out(whole=True)
        mean_square()
        split_ahead(norm_half(2))
        scale_rows(2)
        ada_rows_out(whole=True)
        ada_mods(1, 4, 5)
        dve.wait_ge(out_kv, 32)
        for g in range(NG):
            for cp in range(4):
                copy_turn(dftn[:, :, 2 * cp:2 * cp + 2, g * P:(g + 1) * P].rearrange("p q c n -> p c q n"),
                          lambda b: b.rearrange("p (c q n) -> p c q n", c=2, q=2))
        ada_rows_out()
        for o in range(KT):
            split_turn((f_r[0][:, o, :], f_r[1][:, o, :]), full()[:, 0:T])
        ada_rows_out()
        ada_mods(1, 6)
        ada_rows_out()
        ada_mods(1, 7)
        residual(1, 2, range(4))
        ada_rows_out()
        ada_mods(1, 8)
        residual(1, 2, range(4, KT))
        ada_mods(1, 9)
        coefs(3)
        mean_square()
        split_ahead(norm_half(3))
        scale_rows(3)
        ada_rows_out(whole=True)
        ada_rows_out()
        ada_mods(1, 10, 11)

        b = full()
        dve.tensor_tensor(logits, b[:, 0:16].rearrange("p (g e) -> p g e", g=NG),
                          router_bias[:].rearrange("p (o e) -> p o e", o=1).to_broadcast([P, NG, EXPERTS]),
                          ALU.add).then_inc(evac_done, 1)
        dve.wait_ge(evac_done, turn[0])
        for g in range(NG):
            last = dve.max(top[:, g, :], logits[:, g, :])
        link(last)
        for g in range(NG):
            last = dve.max_index(idx[:, g, :], top[:, g, :], logits[:, g, :])
        link(last)
        dve.tensor_tensor(gap.rearrange("p (g o) -> p g o", o=1), top[:, :, 1:2], top[:, :, 0:1],
                          ALU.subtract).then_inc(gap_ready, 1)
        link(dve.tensor_copy(idx_f, idx[:]))
        for g in range(NG):
            dve.tensor_scalar(hot_1[:, g, :], C("expert_ids"), idx_f[:, g, 0:1], None, ALU.is_equal)
            last = dve.tensor_scalar(hot_2[:, g, :], C("expert_ids"), idx_f[:, g, 1:2], None, ALU.is_equal)
        link(last)
        dve.tensor_tensor(chosen, hot_1, hot_2, ALU.add).then_inc(chosen_ready, 1)
        dve.wait_ge(hi_done, N_SPLIT + 1)
        dve.tensor_tensor(w_lo[:, N_SPLIT % STAGE, :], raw[:, N_PRE % RAW, :], w_hi[:, N_SPLIT % STAGE, :].bitcast(F32),
                          ALU.subtract).then_inc(lo_done, 1)
        b = full()
        dve.tensor_copy(counts, b[:, 16:24]).then_inc(acc_added, CREDIT)
        dve.tensor_copy(rank, b[:, 0:16].rearrange("p (g e) -> p g e", g=NG)).then_inc(evac_done, 1)
        dve.wait_ge(evac_done, turn[0])
        link(dve.reduce_max(most_f, counts, AX_X))
        dve.tensor_copy(most[:], most_f).then_inc(most_ready, 1)

        def build_take(e):
            for g in range(NG):
                last = dve.tensor_scalar(take[:, g, :], C("slot_ids"), rank[:, g, bass.ds(e, 1)],
                                         chosen[:, g, bass.ds(e, 1)], ALU.is_equal, ALU.mult)
            last.then_inc(take_built, 1)

        def hg_remainder(job, q):
            dve.wait_ge(hg_hi, 2 * job + q + 1)
            dst = hg_r[1][:, 4 * q:4 * q + 4, :]
            dve.tensor_tensor(dst, ps[:, 6 + q, :].rearrange("p (c s) -> p c s", c=4),
                              hg_r[0][:, 4 * q:4 * q + 4, :].bitcast(F32), ALU.subtract).then_inc(hg_lo, 1)

        def split_half(job, i):
            m, slot = N_PRE + i, (N_SPLIT + i) % STAGE
            dve.wait_ge(hi_done, N_SPLIT + i + 1 + MOE_HALVES * job)
            dve.tensor_tensor(w_lo[:, slot, :], raw[:, m % RAW, :], w_hi[:, slot, :].bitcast(F32),
                              ALU.subtract).then_inc(lo_done, 1)

        def moe_add(c, src, signal):
            for g in range(NG):
                sl = slice(g * P, (g + 1) * P)
                last = dve.scalar_tensor_tensor(xT[:, c, sl], src[:, sl], mods[:, 1, 40 + c, g:g + 1], xT[:, c, sl],
                                                ALU.mult, ALU.add)
                if g == 0 and signal:
                    last.then_inc(signal, 1)
            return last

        def expert(job, e, last_one=False):
            at = [STAGE]

            def split_to(n):
                while at[0] < n:
                    split_half(job, at[0])
                    at[0] += 1

            def gate(s):
                dve.wait_ge(e_silu, MOE_SLICES * job + s + 1)
                dve.wait_ge(e_used, MOE_HALVES * job + MOE_PLAN.index(("w3", s, 1)) + 1 + CREDIT)
                dve.tensor_tensor(moe_g[:, s % 2, :], ps[:, 3 + 2 * (s % 2), :], moe_silu[:, s % 2, :],
                                  ALU.mult).then_inc(e_g, 1)

            def gt_remainder(s):
                dve.wait_ge(gt_hi, MOE_SLICES * job + s + 1)
                dve.tensor_tensor(gt_r[1][:, s % 2, :, :], ps[:, 6 + s % 2, :].rearrange("p (f s) -> p f s", f=4),
                                  gt_r[0][:, s % 2, :, :].bitcast(F32), ALU.subtract).then_inc(gt_lo, 1)

            if not last_one:
                build_take(e + 1)
            split_to(6)
            gate(0)
            for s in range(1, MOE_SLICES):
                base = MOE_PLAN.index(("w1", s, 0))
                split_to(base + 4)
                gt_remainder(s - 1)
                split_to(base + 6)
                gate(s)
            if not last_one:
                hg_remainder(job + 1, 0)
                hg_remainder(job + 1, 1)
            for g in range(NG):
                last = dve.tensor_scalar(give[:, g, :], C("slot_ids"), rank[:, g, bass.ds(e, 1)],
                                         gates[:, g, bass.ds(e, 1)], ALU.is_equal, ALU.mult)
            last.then_inc(give_built, 1)
            split_to(MOE_HALVES - 1)
            gt_remainder(MOE_SLICES - 1)
            split_to(MOE_HALVES)
            if not last_one:
                split_half(job + 1, 0)
                split_half(job + 1, 1)
                for q in range(4):
                    a = acc[:, 2 * q:2 * q + 2, :]
                    dve.wait_ge(e_spread, 4 * job + q + 1)
                    dve.tensor_tensor(a, ps[:, 2 + q, :].rearrange("p (c t) -> p c t", c=2), a,
                                      ALU.add).then_inc(acc_added, 1)
                split_half(job + 1, 2)
            else:
                dve.wait_ge(acc_added, 4 * job + CREDIT)
                for c in range(KT):
                    last = moe_add(c, acc[:, c, :], None)
                last.then_inc(x_sum, 1)
                dve.wait_ge(x_sum, (job + 1) // EXPERTS)
                for q in range(4):
                    dve.wait_ge(e_spread, 4 * job + q + 1)
                    for i in range(2):
                        moe_add(2 * q + i, ps[:, 2 + q, i * T:(i + 1) * T],
                                None if i else acc_added).then_inc(moe_added, 1)

        dve.wait_ge(acc_zero, 1)
        build_take(0)
        dve.wait_ge(gap_exp_done, 1)
        link(dve.tensor_scalar(gate_den, gap_exp, 1.0, None, ALU.add))
        link(dve.reciprocal(gate_1, gate_den))
        link(dve.tensor_tensor(gate_2, gate_1, gap_exp, ALU.mult))
        for g in range(NG):
            last = dve.tensor_scalar(gates[:, g, :], hot_1[:, g, :], gate_1[:, g:g + 1], None, ALU.mult)
        link(last)
        for g in range(NG):
            last = dve.scalar_tensor_tensor(gates[:, g, :], hot_2[:, g, :], gate_2[:, g:g + 1], gates[:, g, :],
                                            ALU.mult, ALU.add)
        link(last)
        for i in range(1, STAGE):
            split_half(0, i)
        for q in range(2):
            hg_remainder(0, q)
        with dve.Fori(0, EXPERTS - 1) as e:
            expert(e, e)
        expert(EXPERTS - 1, EXPERTS - 1, last_one=True)
        most_here = dve.value_load(most[0:1, 0:1], min_val=0, max_val=T)
        with dve.If(most_here > SLOTS):
            dve.tensor_scalar(rank, rank, -float(SLOTS), None, ALU.add).then_inc(rank_moved, 1)
            dve.memset(acc, 0.0).then_inc(acc_again, 1)
            dve.wait_ge(rank_moved, 1)
            build_take(0)
            for i in range(STAGE):
                split_half(EXPERTS, i)
            for q in range(2):
                hg_remainder(EXPERTS, q)
            dve.wait_ge(acc_again, 1)
            with dve.Fori(0, EXPERTS - 1) as e:
                expert(e + EXPERTS, e)
            expert(2 * EXPERTS - 1, EXPERTS - 1, last_one=True)
        mean_square()
        scale_rows(4)


def shape_constants():
    import numpy as np

    table, dft = np.zeros((P, CONST_N), np.float32), np.zeros((P, DFT_N), np.float32)

    def put(name, a):
        out, (lo, hi) = (table, CONST_AT[name]) if name in CONST_AT else (dft, DFT_AT[name])
        out[:a.shape[0], lo:hi] = a.reshape(a.shape[0], hi - lo)

    i = np.arange(P)
    put("ident", np.eye(P))
    put("pair_sum", np.tile(np.eye(NG), (2, 1)))
    put("ones", np.ones((P, P)))
    col = i % GRID_W
    start = np.clip(col - WIN_COLS // 2, 0, GRID_W - WIN_COLS)[:, None]
    put("mask", np.where((col[None, :] >= start) & (col[None, :] < start + WIN_COLS), 0.0, NEG))
    put("earlier", i[:, None] < i[None, :])
    put("slot_ids", np.tile(np.arange(SLOTS), (P, 1)))
    put("expert_ids", np.tile(np.arange(EXPERTS), (P, 1)))
    u = np.arange(2 * GRID_W - 1)
    z = (np.arange(BIAS_COLS)[:, None] + u[None, :] == WIN_COLS - 1 + GRID_W - 1).astype(np.float32)
    put("diag", z)
    angle = 2 * np.pi * (np.outer(i, i) % P) / P
    put("dft_pos", np.concatenate([np.cos(angle), np.sin(angle)], 1))
    j = np.arange(FGC)
    angle = 2 * np.pi * (np.outer(j, j) % FGC) / FGC
    norm = 1.0 / np.sqrt(P * FGC)
    put("dft_cos", (norm * np.cos(angle)).reshape(2, P, FGC).transpose(1, 0, 2))
    put("dft_sin", (-norm * np.sin(angle)).reshape(2, P, FGC).transpose(1, 0, 2))
    return table, dft


_INS = ["x_prompt", "x_sample", "c", "cache_k", "cache_v", "c_ctx", "ada_w", "ada_b", "norm1_g", "norm2_g", "w_in",
        "conv_w", "rpb", "w_out", "ffn_w1", "ffn_w3", "ffn_w2", "fourier_w", "router_w", "router_b", "moe_w1",
        "moe_w3", "moe_w2", "final_g"]
_OUTS = [((1, P, D), "float32"), ((1, P, D), "float32"), ((1, 1, HEADS, P, HD), "float32"),
         ((1, 1, HEADS, P, HD), "float32")]


def kernel(**inputs):
    import numpy as _np
    import concourse.bacc as _bacc
    from concourse import mybir as _mybir
    from concourse.bass_utils import run_bass_kernel_spmd as _run

    nc = _bacc.Bacc("TRN2", target_bir_lowering=False, num_devices=1)
    arrays, ins, outs = {}, {}, []
    for name in _INS:
        a = _np.ascontiguousarray(inputs[name])
        arrays[f"in_{name}"] = a
        ins[name] = nc.dram_tensor(f"in_{name}", a.shape, _mybir.dt.from_np(a.dtype), kind="ExternalInput").ap()
    tables = []
    for name, table in zip(("shape_constants", "dft_constants"), shape_constants()):
        arrays[name] = table
        tables.append(nc.dram_tensor(name, table.shape, _mybir.dt.float32, kind="ExternalInput").ap())
    for i, (shape, dtype) in enumerate(_OUTS):
        dt = _mybir.dt.from_np(_np.dtype(dtype))
        outs.append(nc.dram_tensor(f"out_{i}", shape, dt, kind="ExternalOutput").ap())
    build(nc, ins, outs, *tables)
    r = _run(nc, [arrays], core_ids=[0])
    return tuple(r.results[0][f"out_{i}"] for i in range(len(_OUTS)))
```
